# Optimizing a Trainium2 kernel written in Bass

```python
import math
import jax
import jax.numpy as jnp
from jax import lax
import numpy as np

D_MODEL = 1024
BATCH = 1
SEQ = 256
DEPTH = 4
DEC_BATCH = 8
DEC_SEQ = 4
PAST_LEN = 256
PAGE_SIZE = 128

N_MIXERS = 3
N_A = (DEPTH + 2) // 3
N_B = (DEPTH + 1) // 3
N_C = DEPTH // 3
D_FF = 2816
NORM_EPS = 1e-6

RWKV_HEAD_DIM = 64
RWKV_HEADS = D_MODEL // RWKV_HEAD_DIM
RWKV_DECAY_LORA = 64
RWKV_AAA_LORA = 64
RWKV_MV_LORA = 32
RWKV_GATE_LORA = 160
RWKV_LNX_EPS = 64e-5

DIFF_HEADS = 8
DIFF_HEAD_DIM = 64
DIFF_E = 2 * DIFF_HEAD_DIM
DIFF_WIDTH = DIFF_HEADS * DIFF_E
SUBLN_EPS = 1e-5
Q_BLOCK = 128
REL_BUCKETS = 32
REL_MAX_EXACT = 16
REL_MAX_DIST = 128

GDN_HEADS = 8
GDN_DK = 128
GDN_DV = 128
GDN_CONV = 4
GDN_CHUNK = 64
GDN_QKV = GDN_HEADS * (2 * GDN_DK + GDN_DV)
GDN_IN = GDN_QKV + GDN_HEADS * GDN_DV + 2 * GDN_HEADS

kernel_name = 'hybrid_rwkv7_diffattn_gdn_macaron_step'

def rmsnorm(x, w, eps=NORM_EPS):
    xf = x.astype(jnp.float32)
    y = xf * lax.rsqrt(jnp.mean(xf * xf, axis=-1, keepdims=True) + eps)
    return (y * w.astype(jnp.float32)).astype(x.dtype)

def l2norm(t, eps):
    return t * lax.rsqrt(jnp.sum(t * t, axis=-1, keepdims=True) + eps)

def macaron_half(x, g, w_gate, w_up, w_down):
    h = rmsnorm(x, g)
    return x + 0.5 * ((jax.nn.silu(h @ w_gate) * (h @ w_up)) @ w_down)

def rwkv7_mix(u, shift_prev, S0, p, v_first, vres):
    B, T, D = u.shape
    H, N = RWKV_HEADS, RWKV_HEAD_DIM
    f32 = jnp.float32
    prev = jnp.concatenate([shift_prev[:, None, :].astype(u.dtype), u[:, :-1]], axis=1)
    xx = prev - u
    mu = p['mu']
    xr, xw, xk = u + xx * mu[0], u + xx * mu[1], u + xx * mu[2]
    xv, xa, xg = u + xx * mu[3], u + xx * mu[4], u + xx * mu[5]
    r = xr @ p['w_rkv'][0]
    k = xk @ p['w_rkv'][1]
    v = xv @ p['w_rkv'][2]
    wlog = -jax.nn.softplus(-(p['w0'] + jnp.tanh(xw @ p['w1']) @ p['w2']).astype(f32)) - 0.5
    decay = jnp.exp(-jnp.exp(wlog))
    if vres is None:
        v_first = v
    else:
        v0, v1, v2 = vres
        v = v + (v_first - v) * jax.nn.sigmoid(v0 + (xv @ v1) @ v2)
    a = jax.nn.sigmoid((p['a0'] + (xa @ p['a1']) @ p['a2']).astype(f32))
    gate = jax.nn.sigmoid(xg @ p['g1']) @ p['g2']

    def heads(t):
        return t.astype(f32).reshape(B, T, H, N)

    kk = l2norm(heads(k * p['k_k']), 1e-24)
    k_mod = k.astype(f32) * (1.0 + (a - 1.0) * p['k_a'].astype(f32))
    r_h, w_h, k_h, v_h, a_h = heads(r), heads(decay), heads(k_mod), heads(v), heads(a)
    seq = tuple(jnp.moveaxis(t, 1, 0) for t in (r_h, w_h, k_h, v_h, -kk, kk * a_h))

    def step(S, inp):
        r_t, w_t, k_t, v_t, a_t, b_t = inp
        sa = jnp.einsum('bhvk,bhk->bhv', S, a_t)
        S = S * w_t[:, :, None, :] + sa[..., None] * b_t[:, :, None, :] + v_t[..., None] * k_t[:, :, None, :]
        return S, jnp.einsum('bhvk,bhk->bhv', S, r_t)

    S, o = lax.scan(step, S0.astype(f32), seq)
    o = jnp.moveaxis(o, 0, 1)
    mean = jnp.mean(o, axis=-1, keepdims=True)
    var = jnp.mean(jnp.square(o - mean), axis=-1, keepdims=True)
    o = ((o - mean) * lax.rsqrt(var + RWKV_LNX_EPS)).reshape(B, T, D)
    o = o * p['lnx_w'].astype(f32) + p['lnx_b'].astype(f32)
    bonus = jnp.sum(r_h * k_h * p['r_k'].astype(f32), axis=-1, keepdims=True) * v_h
    o = (o + bonus.reshape(B, T, D)).astype(u.dtype) * gate
    return o @ p['w_o'], v_first, S, u[:, -1]

def t5_bucket(q_pos, k_pos):
    n = jnp.maximum(q_pos[:, None] - k_pos[None, :], 0)
    nf = jnp.maximum(n, 1).astype(jnp.float32)
    large = REL_MAX_EXACT + (jnp.log(nf / REL_MAX_EXACT) / math.log(REL_MAX_DIST / REL_MAX_EXACT)
                             * (REL_BUCKETS - REL_MAX_EXACT)).astype(jnp.int32)
    large = jnp.minimum(large, REL_BUCKETS - 1)
    return jnp.where(n < REL_MAX_EXACT, n, large)

def diff_sweep(q, k, v, q_pos, k_pos, lam, rel_bias):
    B, T, H, E = q.shape
    dh = E // 2
    qb = math.gcd(T, Q_BLOCK)
    nb = T // qb
    scale = dh ** -0.5
    kf = k.astype(jnp.float32)
    k1, k2 = kf[..., :dh], kf[..., dh:]
    vf = v.astype(jnp.float32)
    table = rel_bias.astype(jnp.float32)
    q_blocks = jnp.moveaxis(q.astype(jnp.float32).reshape(B, nb, qb, H, E), 1, 0)
    pos_blocks = q_pos.reshape(nb, qb)

    def one_block(args):
        qblk, qp = args
        bias = jnp.moveaxis(table[t5_bucket(qp, k_pos)], -1, 0)
        visible = k_pos[None, :] <= qp[:, None]
        s1 = jnp.einsum('bqhd,bshd->bhqs', qblk[..., :dh], k1) * scale + bias
        s2 = jnp.einsum('bqhd,bshd->bhqs', qblk[..., dh:], k2) * scale + bias
        p1 = jax.nn.softmax(jnp.where(visible, s1, -jnp.inf), axis=-1)
        p2 = jax.nn.softmax(jnp.where(visible, s2, -jnp.inf), axis=-1)
        return jnp.einsum('bhqs,bshe->bqhe', p1 - lam * p2, vf)

    o = lax.map(one_block, (q_blocks, pos_blocks))
    return jnp.moveaxis(o, 0, 1).reshape(B, T, H, E)

def diff_attention_mix(u, past_k, past_v, p, lam_init, rel_bias):
    B, T, _ = u.shape
    H, E = DIFF_HEADS, DIFF_E
    q, k, v = jnp.split(u @ p['w_qkv'], 3, axis=-1)
    q, k, v = q.reshape(B, T, H, E), k.reshape(B, T, H, E), v.reshape(B, T, H, E)
    if past_k is None:
        k_all, v_all = k, v
    else:
        k_all = jnp.concatenate([past_k.astype(k.dtype), k], axis=1)
        v_all = jnp.concatenate([past_v.astype(v.dtype), v], axis=1)
    past = k_all.shape[1] - T
    q_pos = past + jnp.arange(T, dtype=jnp.int32)
    k_pos = jnp.arange(past + T, dtype=jnp.int32)
    lv = p['lam'].astype(jnp.float32)
    lam = jnp.exp(jnp.sum(lv[0] * lv[1])) - jnp.exp(jnp.sum(lv[2] * lv[3])) + lam_init
    o = diff_sweep(q, k_all, v_all, q_pos, k_pos, lam, rel_bias)
    o = rmsnorm(o, p['subln_w'], SUBLN_EPS) * (1.0 - lam_init)
    return o.astype(u.dtype).reshape(B, T, H * E) @ p['w_o'], k, v

def gated_delta_chunked(q, k, v, beta, g, S0):
    B, T, H, DK = q.shape
    DV = v.shape[-1]
    L = math.gcd(T, GDN_CHUNK)
    n = T // L

    def to_chunks(t):
        t = t.reshape((B, n, L) + t.shape[2:])
        return jnp.moveaxis(jnp.moveaxis(t, 1, 0), 2, 3)

    qc, kc, vc, bc, gc = (to_chunks(t) for t in (q, k, v, beta, g))
    gc = jnp.cumsum(gc, axis=-1)
    diff = gc[..., :, None] - gc[..., None, :]
    idx = jnp.arange(L)
    strict = idx[:, None] > idx[None, :]
    incl = idx[:, None] >= idx[None, :]
    decay_strict = jnp.exp(jnp.where(strict, diff, -jnp.inf))
    decay_incl = jnp.exp(jnp.where(incl, diff, -jnp.inf))
    a_mat = bc[..., :, None] * jnp.einsum('nbhid,nbhjd->nbhij', kc, kc) * decay_strict + jnp.eye(L, dtype=q.dtype)
    rhs = jnp.concatenate([bc[..., None] * vc, (bc * jnp.exp(gc))[..., None] * kc], axis=-1)
    sol = lax.linalg.triangular_solve(a_mat, rhs, left_side=True, lower=True, unit_diagonal=True)
    wv, wk = sol[..., :DV], sol[..., DV:]
    aqk = jnp.einsum('nbhid,nbhjd->nbhij', qc, kc) * decay_incl
    qg = qc * jnp.exp(gc)[..., None]
    kd = kc * jnp.exp(gc[..., -1:] - gc)[..., None]
    glast = jnp.exp(gc[..., -1])

    def step(S, c):
        wv_c, wk_c, aqk_c, qg_c, kd_c, gl_c = c
        u = wv_c - jnp.einsum('bhlk,bhkv->bhlv', wk_c, S)
        o = jnp.einsum('bhlk,bhkv->bhlv', qg_c, S) + jnp.einsum('bhij,bhjv->bhiv', aqk_c, u)
        S = gl_c[..., None, None] * S + jnp.einsum('bhlk,bhlv->bhkv', kd_c, u)
        return S, o

    S, o = lax.scan(step, S0, (wv, wk, aqk, qg, kd, glast))
    o = jnp.swapaxes(jnp.moveaxis(o, 0, 1), 2, 3).reshape(B, T, H, DV)
    return o, S

def gdn_mix(u, conv_prev, S0, p):
    B, T, _ = u.shape
    H, DK, DV = GDN_HEADS, GDN_DK, GDN_DV
    f32 = jnp.float32
    proj = u @ p['w_in']
    qkv = proj[..., :GDN_QKV]
    z = proj[..., GDN_QKV:GDN_QKV + H * DV]
    b_raw = proj[..., GDN_QKV + H * DV:GDN_QKV + H * DV + H]
    a_raw = proj[..., GDN_QKV + H * DV + H:]
    xp = jnp.concatenate([conv_prev.astype(u.dtype), qkv], axis=1)
    conv = sum(p['conv_w'][j] * xp[:, j:j + T] for j in range(GDN_CONV))
    qkv_c = jax.nn.silu(conv).astype(f32)
    q = l2norm(qkv_c[..., :H * DK].reshape(B, T, H, DK), 1e-6) * (DK ** -0.5)
    k = l2norm(qkv_c[..., H * DK:2 * H * DK].reshape(B, T, H, DK), 1e-6)
    v = qkv_c[..., 2 * H * DK:].reshape(B, T, H, DV)
    beta = jax.nn.sigmoid(b_raw.astype(f32))
    g = -jnp.exp(p['a_log'].astype(f32)) * jax.nn.softplus(a_raw.astype(f32) + p['dt_bias'].astype(f32))
    o, S = gated_delta_chunked(q, k, v, beta, g, S0.astype(f32))
    o = rmsnorm(o, p['norm_w']) * jax.nn.silu(z.astype(f32).reshape(B, T, H, DV))
    out = o.astype(u.dtype).reshape(B, T, H * DV) @ p['w_o']
    return out, S, xp[:, -(GDN_CONV - 1):]

def setup_inputs(seed: int = 0) -> dict:
    key = jax.random.key(seed)
    keys = list(jax.random.split(key, 64))
    f32 = jnp.float32

    def nk():
        return keys.pop()

    def dense(shape, fan_in, scale=1.0):
        return jax.random.normal(nk(), shape, f32) * (scale / math.sqrt(fan_in))

    def small(shape, scale):
        return scale * jax.random.normal(nk(), shape, f32)

    def gain(shape, center=1.0):
        return center + 0.05 * jax.random.normal(nk(), shape, f32)

    n_pages = PAST_LEN // PAGE_SIZE
    n_used = DEC_BATCH * n_pages
    n_pool = n_used + max(1, n_used // 4)
    page_table = jax.random.permutation(nk(), n_pool)[:n_used].reshape(DEC_BATCH, n_pages).astype(jnp.int32)
    dt = jnp.exp(jax.random.uniform(nk(), (N_C, GDN_HEADS), f32, math.log(1e-3), math.log(1e-1)))
    nv = max(N_A - 1, 0)
    return {
        'x_prompt': small((BATCH, SEQ, D_MODEL), 1.0),
        'x_sample': small((DEC_BATCH, DEC_SEQ, D_MODEL), 1.0),
        'state_rwkv_wkv': small((N_A, DEC_BATCH, RWKV_HEADS, RWKV_HEAD_DIM, RWKV_HEAD_DIM), 0.5),
        'state_rwkv_shift': small((N_A, DEC_BATCH, D_MODEL), 1.0),
        'cache_attn_k': small((N_B, n_pool, PAGE_SIZE, DIFF_HEADS, DIFF_E), 1.0),
        'cache_attn_v': small((N_B, n_pool, PAGE_SIZE, DIFF_HEADS, DIFF_E), 1.0),
        'state_gdn': small((N_C, DEC_BATCH, GDN_HEADS, GDN_DK, GDN_DV), 0.1),
        'state_gdn_conv': small((N_C, DEC_BATCH, GDN_CONV - 1, GDN_QKV), 1.0),
        'page_table': page_table,
        'norm_w': gain((DEPTH, 3, D_MODEL)),
        'final_norm_w': gain((D_MODEL,)),
        'ffn_w_gate': dense((DEPTH, 2, D_MODEL, D_FF), D_MODEL),
        'ffn_w_up': dense((DEPTH, 2, D_MODEL, D_FF), D_MODEL),
        'ffn_w_down': dense((DEPTH, 2, D_FF, D_MODEL), D_FF),
        'rwkv_mu': jax.random.uniform(nk(), (N_A, 6, D_MODEL), f32),
        'rwkv_w_rkv': dense((N_A, 3, D_MODEL, D_MODEL), D_MODEL),
        'rwkv_w_o': dense((N_A, D_MODEL, D_MODEL), D_MODEL),
        'rwkv_w0': jax.random.uniform(nk(), (N_A, D_MODEL), f32, -6.0, -0.5),
        'rwkv_w1': dense((N_A, D_MODEL, RWKV_DECAY_LORA), D_MODEL),
        'rwkv_w2': dense((N_A, RWKV_DECAY_LORA, D_MODEL), RWKV_DECAY_LORA, 0.5),
        'rwkv_a0': small((N_A, D_MODEL), 0.1),
        'rwkv_a1': dense((N_A, D_MODEL, RWKV_AAA_LORA), D_MODEL),
        'rwkv_a2': dense((N_A, RWKV_AAA_LORA, D_MODEL), RWKV_AAA_LORA, 0.5),
        'rwkv_g1': dense((N_A, D_MODEL, RWKV_GATE_LORA), D_MODEL),
        'rwkv_g2': dense((N_A, RWKV_GATE_LORA, D_MODEL), RWKV_GATE_LORA),
        'rwkv_k_k': gain((N_A, D_MODEL), 0.85),
        'rwkv_k_a': gain((N_A, D_MODEL), 1.0),
        'rwkv_r_k': gain((N_A, RWKV_HEADS, RWKV_HEAD_DIM), -0.04),
        'rwkv_lnx_w': gain((N_A, D_MODEL)),
        'rwkv_lnx_b': small((N_A, D_MODEL), 0.02),
        'rwkv_v0': gain((nv, D_MODEL), 1.0),
        'rwkv_v1': dense((nv, D_MODEL, RWKV_MV_LORA), D_MODEL),
        'rwkv_v2': dense((nv, RWKV_MV_LORA, D_MODEL), RWKV_MV_LORA, 0.5),
        'attn_w_qkv': dense((N_B, D_MODEL, 3 * DIFF_WIDTH), D_MODEL),
        'attn_w_o': dense((N_B, DIFF_WIDTH, D_MODEL), DIFF_WIDTH),
        'attn_lambda': small((N_B, 4, DIFF_HEAD_DIM), 0.1),
        'attn_subln_w': gain((N_B, DIFF_E)),
        'rel_bias': small((REL_BUCKETS, DIFF_HEADS), 0.5),
        'gdn_w_in': dense((N_C, D_MODEL, GDN_IN), D_MODEL),
        'gdn_conv_w': small((N_C, GDN_CONV, GDN_QKV), 0.5),
        'gdn_a_log': jnp.log(jax.random.uniform(nk(), (N_C, GDN_HEADS), f32, 1.0, 16.0)),
        'gdn_dt_bias': dt + jnp.log(-jnp.expm1(-dt)),
        'gdn_norm_w': gain((N_C, GDN_DV)),
        'gdn_w_o': dense((N_C, GDN_HEADS * GDN_DV, D_MODEL), GDN_HEADS * GDN_DV),
    }

def reference(x_prompt, x_sample, state_rwkv_wkv, state_rwkv_shift, cache_attn_k, cache_attn_v,
              state_gdn, state_gdn_conv, page_table, norm_w, final_norm_w, ffn_w_gate, ffn_w_up,
              ffn_w_down, rwkv_mu, rwkv_w_rkv, rwkv_w_o, rwkv_w0, rwkv_w1, rwkv_w2, rwkv_a0, rwkv_a1,
              rwkv_a2, rwkv_g1, rwkv_g2, rwkv_k_k, rwkv_k_a, rwkv_r_k, rwkv_lnx_w, rwkv_lnx_b, rwkv_v0,
              rwkv_v1, rwkv_v2, attn_w_qkv, attn_w_o, attn_lambda, attn_subln_w, rel_bias, gdn_w_in,
              gdn_conv_w, gdn_a_log, gdn_dt_bias, gdn_norm_w, gdn_w_o):
    B = x_prompt.shape[0]
    DB = x_sample.shape[0]
    dt = x_prompt.dtype
    xp, xs = x_prompt, x_sample
    vf_p = vf_s = None
    wkv_p, shift_p, ak_p, av_p, gs_p, gc_p = [], [], [], [], [], []
    wkv_s, shift_s, ak_s, av_s, gs_s, gc_s = [], [], [], [], [], []
    for i in range(DEPTH):
        kind, j = i % N_MIXERS, i // N_MIXERS
        fa = (norm_w[i, 0], ffn_w_gate[i, 0], ffn_w_up[i, 0], ffn_w_down[i, 0])
        fb = (norm_w[i, 2], ffn_w_gate[i, 1], ffn_w_up[i, 1], ffn_w_down[i, 1])
        xp = macaron_half(xp, *fa)
        xs = macaron_half(xs, *fa)
        up = rmsnorm(xp, norm_w[i, 1])
        us = rmsnorm(xs, norm_w[i, 1])
        if kind == 0:
            p = dict(mu=rwkv_mu[j], w_rkv=rwkv_w_rkv[j], w_o=rwkv_w_o[j], w0=rwkv_w0[j], w1=rwkv_w1[j],
                     w2=rwkv_w2[j], a0=rwkv_a0[j], a1=rwkv_a1[j], a2=rwkv_a2[j], g1=rwkv_g1[j], g2=rwkv_g2[j],
                     k_k=rwkv_k_k[j], k_a=rwkv_k_a[j], r_k=rwkv_r_k[j], lnx_w=rwkv_lnx_w[j], lnx_b=rwkv_lnx_b[j])
            vres = None if j == 0 else (rwkv_v0[j - 1], rwkv_v1[j - 1], rwkv_v2[j - 1])
            zero_shift = jnp.zeros((B, D_MODEL), up.dtype)
            zero_state = jnp.zeros((B, RWKV_HEADS, RWKV_HEAD_DIM, RWKV_HEAD_DIM), jnp.float32)
            mp, vf_p, s_p, sh_p = rwkv7_mix(up, zero_shift, zero_state, p, vf_p, vres)
            ms, vf_s, s_s, sh_s = rwkv7_mix(us, state_rwkv_shift[j], state_rwkv_wkv[j], p, vf_s, vres)
            wkv_p.append(s_p.astype(dt)); shift_p.append(sh_p.astype(dt))
            wkv_s.append(s_s.astype(dt)); shift_s.append(sh_s.astype(dt))
        elif kind == 1:
            p = dict(w_qkv=attn_w_qkv[j], w_o=attn_w_o[j], lam=attn_lambda[j], subln_w=attn_subln_w[j])
            lam_init = 0.8 - 0.6 * math.exp(-0.3 * i)
            mp, k_p, v_p = diff_attention_mix(up, None, None, p, lam_init, rel_bias)
            past_k = cache_attn_k[j][page_table].reshape(DB, -1, DIFF_HEADS, DIFF_E)
            past_v = cache_attn_v[j][page_table].reshape(DB, -1, DIFF_HEADS, DIFF_E)
            ms, k_s, v_s = diff_attention_mix(us, past_k, past_v, p, lam_init, rel_bias)
            ak_p.append(k_p); av_p.append(v_p)
            ak_s.append(k_s); av_s.append(v_s)
        else:
            p = dict(w_in=gdn_w_in[j], conv_w=gdn_conv_w[j], a_log=gdn_a_log[j], dt_bias=gdn_dt_bias[j],
                     norm_w=gdn_norm_w[j], w_o=gdn_w_o[j])
            zero_conv = jnp.zeros((B, GDN_CONV - 1, GDN_QKV), up.dtype)
            zero_state = jnp.zeros((B, GDN_HEADS, GDN_DK, GDN_DV), jnp.float32)
            mp, s_p, c_p = gdn_mix(up, zero_conv, zero_state, p)
            ms, s_s, c_s = gdn_mix(us, state_gdn_conv[j], state_gdn[j], p)
            gs_p.append(s_p.astype(dt)); gc_p.append(c_p.astype(dt))
            gs_s.append(s_s.astype(dt)); gc_s.append(c_s.astype(dt))
        xp = xp + mp
        xs = xs + ms
        xp = macaron_half(xp, *fb)
        xs = macaron_half(xs, *fb)
    y_prompt = rmsnorm(xp, final_norm_w)
    y_sample = rmsnorm(xs, final_norm_w)
    return (y_prompt, y_sample,
            jnp.stack(wkv_p), jnp.stack(shift_p), jnp.stack(ak_p), jnp.stack(av_p), jnp.stack(gs_p), jnp.stack(gc_p),
            jnp.stack(wkv_s), jnp.stack(shift_s), jnp.stack(ak_s), jnp.stack(av_s), jnp.stack(gs_s), jnp.stack(gc_s))


_drawn_inputs = setup_inputs


def setup_inputs(seed=0):
    import zlib

    import numpy as np

    out = dict(_drawn_inputs(seed))
    spreads = {}
    factors = {'rwkv_v0': 40.032, 'gdn_norm_w': 2.675, 'rwkv_v1': 8.0, 'rwkv_v2': 8.0}
    for name, (base, spread) in spreads.items():
        noise = np.random.default_rng([zlib.crc32(name.encode()), seed]).standard_normal(out[name].shape)
        drawn = base * np.exp(spread * noise) if base else spread * noise
        out[name] = jnp.asarray(drawn.astype(out[name].dtype))
    for name, factor in factors.items():
        out[name] = (out[name] * factor).astype(out[name].dtype)
    return out
```

```python
import math
import numpy as np
import concourse.bass as bass
from concourse import mybir
from contextlib import ExitStack

D = 1024
SEQ = 256
DEC_B, DEC_T = 8, 4
NS = DEC_B * DEC_T
NT = SEQ + NS
CH = D // 128
DFF = 2816
FCH = DFF // 128
DEPTH = 4
EPS = 1e-6
SLOTS = 4
GU_UNITS = FCH // 2
DN_UNITS = 8
FFN_UNITS = GU_UNITS + DN_UNITS
PIECES = 2 * FFN_UNITS
PARTS = CH + FCH
TOK_TILES = [(0, 128), (128, 128), (256, NS)]
RH = 16
DE = 64
RC = 64
GH = 8
GROUP = 4
LEVELS = 7


def constant_table():
    m = np.arange(128)[:, None]
    n = np.arange(128)[None, :]
    parts, at = {}, 0
    cols = []

    def put(name, a):
        nonlocal at
        a = np.asarray(a, np.float32)
        full = np.zeros((128, a.shape[1]), np.float32)
        full[:a.shape[0]] = a
        cols.append(full)
        parts[name] = (at, at + a.shape[1])
        at += a.shape[1]

    put("ident", m == n)
    put("ones", np.ones((128, 128)))
    put("blk64", m // DE == n // DE)
    put("strict64", (n > m) & (m // RC == n // RC))
    put("incl64", (n >= m) & (m // RC == n // RC))
    put("strict4", ((n > m) & (m // DEC_T == n // DEC_T))[:NS, :NS])
    put("incl4", ((n >= m) & (m // DEC_T == n // DEC_T))[:NS, :NS])
    for i in range(LEVELS):
        b = 2 ** i
        put(f"level{i}", (n // b == m // b + 1) & (n // b % 2 == 1))
    reset = np.ones(NT)
    reset[0:SEQ:RC] = 0
    reset[SEQ::DEC_T] = 0
    put("reset", np.broadcast_to(reset, (128, NT)))
    put("strict128", n > m)
    put("incl128", n >= m)
    put("after128", n < m)
    put("after4", ((n < m) & (m // DEC_T == n // DEC_T))[:NS, :NS])
    put("same4", (m // DEC_T == n // DEC_T)[:NS, :NS])
    put("seq4", (np.arange(NS)[:, None] // DEC_T == np.arange(DEC_B)[None, :]))
    return np.concatenate(cols, 1), parts


CONST_ARRAY, CONST_COLS = constant_table()

AH = 8
PAST = 256
PAGE = 128
BUCKETS = 32
NEG = -1e30
FAR = PAST + DEC_T - 1
FN = FAR + 1 + 128
SK = PAST + NS
LAM_INIT = 0.8 - 0.6 * math.exp(-0.3)


def bucket_of(n):
    n = np.asarray(n)
    nf = np.maximum(n, 1).astype(np.float32)
    large = 16 + (np.log(nf / 16) / math.log(128 / 16) * 16).astype(np.int32)
    return np.where(n < 16, n, np.minimum(large, BUCKETS - 1))


def attention_constants():
    parts, cols, at = {}, [], 0

    def put(name, a):
        nonlocal at
        full = np.zeros((128, a.shape[1]), np.float32)
        full[:a.shape[0]] = a
        cols.append(full)
        parts[name] = (at, at + a.shape[1])
        at += a.shape[1]

    m = np.arange(FN) - FAR
    one = np.zeros((BUCKETS + 1, FN))
    one[np.where(m <= 0, bucket_of(np.maximum(-m, 0)), BUCKETS), np.arange(FN)] = 1
    put("by_distance", one)
    for i in range(DEC_T):
        key = np.arange(SK)
        new = (key - PAST) % DEC_T
        dist = np.where(key < PAST, PAST + i - key, i - new)
        one = np.zeros((BUCKETS + 1, SK))
        one[np.where(dist >= 0, bucket_of(np.maximum(dist, 0)), BUCKETS), key] = 1
        put(f"sample{i}", one)
    row = np.arange(128)
    for r in range(4):
        own = (2 * r + row // 64)[:, None] == (np.arange(NS) // DEC_T)[None, :]
        put(f"other{r}", np.where(own, 0, NEG))
    put("flip", np.eye(128)[::-1])
    put("half0", (row // 4 % 2 == 0)[:, None].astype(np.float32))
    put("half1", (row // 4 % 2 == 1)[:, None].astype(np.float32))
    return np.concatenate(cols, 1), parts


ATTN_ARRAY, ATTN_COLS = attention_constants()


def program(nc, t, stages):
    f32 = mybir.dt.float32
    ALU = mybir.AluOpType
    ACT = mybir.ActivationFunctionType
    AX = mybir.AxisListType
    ctx = ExitStack()
    with ctx:
        def sb(name, shape, dt=f32):
            return ctx.enter_context(nc.sbuf_tensor(name, shape, dt))

        def sem(name):
            return ctx.enter_context(nc.semaphore(name))

        x = sb("x", [128, CH, NT])
        h = sb("h", [128, CH, NT])
        ring = sb("ring", [128, SLOTS, 4096])
        work_at = nc.sbuf_base
        work = sb("work", [128, 12, CH, NT])
        wflat = work[:, :, :, :].rearrange("p a c n -> p (a c n)")

        silu = wflat[:, 2 * FCH * NT:(2 * FCH + 2) * NT].rearrange("p (f n) -> p f n", n=NT)
        prod = wflat[:, (2 * FCH + 2) * NT:(2 * FCH + 4) * NT].rearrange("p (f n) -> p f n", n=NT)

        def part(name, at, shape):
            return nc.alloc_sbuf_tensor_at(name, [128] + shape, mybir.dt.float32r, offset=work_at + 4 * at)

        hid_hi = part("hid_hi", 0, [FCH, NT])
        hid_lo = part("hid_lo", FCH * NT, [FCH, NT])
        w_at = (2 * FCH + 4) * NT
        w_hi = [part(f"w_hi{i}", w_at + 4096 * i, [2 * CH, 128]) for i in range(2)]
        w_lo = [part(f"w_lo{i}", w_at + 4096 * i + 2048, [2 * CH, 128]) for i in range(2)]
        h_hi = part("h_hi", w_at + 8192, [CH, NT])
        h_lo = part("h_lo", w_at + 8192 + CH * NT, [CH, NT])
        prm_rows = wflat[:, 24 * NT:24 * NT + 512].rearrange("p (k q) -> p k q", q=128)
        rms = sb("rms", [128, NT])
        rinv = sb("rinv", [128, NT])
        consts = sb("consts", [128, CONST_ARRAY.shape[1]])

        def const(name, p=128, n=None):
            a, b = CONST_COLS[name]
            return consts[0:p, a:b if n is None else a + n]

        ident = const("ident")
        ones = const("ones")
        eps_col = sb("eps_col", [128, 4])
        prm = sb("prm", [128, 512])
        bank = [ctx.enter_context(nc.psum_tensor(f"bank{i}", [128, 512], f32)) for i in range(8)]

        xin = wflat[:, 0:3 * D].rearrange("p (t d) -> p t d", t=3)
        yout = xin

        consts_in = sem("consts_in")
        consts_set = sem("consts_set")
        x_in = sem("x_in")
        prm_transposed = sem("prm_transposed")
        prm_ready = sem("prm_ready")
        x_transposed = sem("x_transposed")
        half_done = sem("half_done")
        slot_full = [sem(f"slot{i}_full") for i in range(SLOTS)]
        gate_up_free = sem("gate_up_free")
        silu_done = sem("silu_done")
        w_hi_ready = sem("w_hi_ready")
        w_lo_ready = sem("w_lo_ready")
        act_hi_ready = sem("act_hi_ready")
        act_lo_ready = sem("act_lo_ready")
        x_updated = sem("x_updated")
        squared = sem("squared")
        ssq_done = sem("ssq_done")
        rms_done = sem("rms_done")
        rinv_done = sem("rinv_done")
        h_ready = sem("h_ready")
        y_transposed = sem("y_transposed")
        y_copied = sem("y_copied")
        stored = sem("stored")

        rows = []
        def vec(ap2d, n):
            at = len(rows)
            rows.extend([(ap2d, i) for i in range(n)])
            return at
        NORM = vec(t["norm_w"].rearrange("l j (c q) -> (l j c) q", q=128), 96)
        FINAL = vec(t["final_norm_w"].rearrange("(c q) -> c q", q=128), 8)
        MU = vec(t["rwkv_mu"].rearrange("j m (c q) -> (j m c) q", q=128), 96)
        W0 = vec(t["rwkv_w0"].rearrange("j (c q) -> (j c) q", q=128), 16)
        A0 = vec(t["rwkv_a0"].rearrange("j (c q) -> (j c) q", q=128), 16)
        KKW = vec(t["rwkv_k_k"].rearrange("j (c q) -> (j c) q", q=128), 16)
        KAW = vec(t["rwkv_k_a"].rearrange("j (c q) -> (j c) q", q=128), 16)
        RKW = vec(t["rwkv_r_k"].rearrange("j (c a) q -> (j c) (a q)", a=2), 16)
        LNW = vec(t["rwkv_lnx_w"].rearrange("j (c q) -> (j c) q", q=128), 16)
        LNB = vec(t["rwkv_lnx_b"].rearrange("j (c q) -> (j c) q", q=128), 16)
        V0 = vec(t["rwkv_v0"].rearrange("j (c q) -> (j c) q", q=128), 8)
        CONVW = vec(t["gdn_conv_w"].rearrange("o j (c q) -> (o j c) q", q=128), 96)
        SUBLN = vec(t["attn_subln_w"], 1)
        GDNN = vec(t["gdn_norm_w"], 1)
        NROWS = len(rows)
        ROW_TILES = [(k, min(128, NROWS - 128 * k)) for k in range(4)]

        units = []
        unit_base = {}

        def square_units(w):
            src = w.rearrange("(k q) n -> q k n", q=128)
            for n0 in range(0, w.shape[1] // 512):
                units.append(([(0, 128, 4, 512, src[:, 0:4, 512 * n0:512 * n0 + 512]),
                               (2048, 128, 4, 512, src[:, 4:8, 512 * n0:512 * n0 + 512])], 2))

        def lora_units(j):
            kq = "(k q) n -> q k n"
            first = [(0, 128, 8, 64, t["rwkv_w1"][j].rearrange(kq, q=128)),
                     (512, 128, 8, 64, t["rwkv_a1"][j].rearrange(kq, q=128)),
                     (1024, 128, 8, 160, t["rwkv_g1"][j].rearrange(kq, q=128))]
            if j > 0:
                first += [(2304, 128, 8, 32, t["rwkv_v1"][j - 1].rearrange(kq, q=128)),
                          (2560, 32, 1, 1024, t["rwkv_v2"][j - 1].unsqueeze(1))]
            units.append((first, 5 if j else 4))
            units.append(([(0, 64, 1, 1024, t["rwkv_w2"][j].unsqueeze(1)),
                           (1024, 64, 1, 1024, t["rwkv_a2"][j].unsqueeze(1)),
                           (2048, 128, 1, 1024, t["rwkv_g2"][j, 0:128].unsqueeze(1)),
                           (3072, 32, 1, 1024, t["rwkv_g2"][j, 128:160].unsqueeze(1))], 32 if j else 24))

        for s, (kind, n) in enumerate(stages):
            unit_base[s] = len(units)
            if kind == "ffn":
                units += [([None, None], 2)] * FFN_UNITS
            elif kind == "gdn":
                src = t["gdn_w_in"][0]
                units.append(([(0, 128, 8, 2 * GH, src[:, 4 * D:].rearrange("(k q) n -> q k n", q=128))], 1))
                square_units(src[:, 0:4 * D])
                square_units(t["gdn_w_o"][0])
            elif kind == "attn":
                square_units(t["attn_w_qkv"][0])
                square_units(t["attn_w_o"][0])
            elif kind == "rwkv":
                lora_units(n)
                for m in (2, 0, 1):
                    square_units(t["rwkv_w_rkv"][n, m])
                square_units(t["rwkv_w_o"][n])

        def HD(unit, halves):
            return 2 * SLOTS + sum(u[1] for u in units[0:max(unit, 0)]) + 2 * min(unit, 0) + halves

        def released(unit):
            if unit >= 0 and len(units[unit][0]) > 2 and units[unit][1] <= 5 :
                unit += 1
            return HD(unit, units[unit][1] if unit >= 0 else 2)

        def full(unit):
            return 16 * sum(len(u[0]) for u in units[unit % SLOTS:unit + 1:SLOTS])

        def split_credit(s):
            return 2 * SLOTS + PIECES * ffn_before[s]

        def W(i):
            return work[:, i]

        def by_feature(at):
            return prm[:, at:at + CH].unsqueeze(2).broadcast_to([128, CH, NT])

        R_, K_, V_, SW_, XX_, GATE_, BONUS_, XM0_, XM1_, A_, SV_, LORA_ = range(12)
        AT_, BT_, KT_, RT_, O_, P_, PI_, KN_ = SW_, XX_, K_, R_, XM0_, XM0_, XM1_, SV_
        lora_h = W(LORA_)
        scr = wflat[:, 8 * CH * NT:12 * CH * NT]
        tokV, tokB, tokK = (scr[:, 1024 * i:1024 * i + 1024] for i in range(3))
        Am = scr[:, 3072:5120].rearrange("p (h k n) -> p h k n", h=4, k=4)
        NL = scr[:, 5120:7680].rearrange("p (l h n) -> p l h n", l=5, h=4)
        Xm = scr[:, 7680:8192].rearrange("p (h n) -> p h n", h=4)
        XT = scr[:, 8192:8704].rearrange("p (h n) -> p h n", h=4)
        Xboth = scr[:, 7680:8704].rearrange("p (w h n) -> p w h n", w=2, h=4)
        Ym = scr[:, 8704:9216].rearrange("p (h n) -> p h n", h=4)
        hflat = h[:, :, :].rearrange("p c n -> p (c n)")
        Rhs = hflat[:, 0:256]
        Um = hflat[:, 256:512]
        Tbd = hflat[:, 512:1536].rearrange("p (c n) -> p c n", n=128)
        PL = hflat[:, 1536:1568].rearrange("p (c n) -> p c n", n=4)
        PLs = hflat[:, 1568:1632].rearrange("p (c n) -> p c n", n=8)
        Tst = hflat[:, 1632:2144].rearrange("p (c n) -> p c n", n=64)
        Ttmp = hflat[:, 2144:2272]
        S0 = NL[0:64, 1:3].rearrange("p l h n -> p (l h n)").rearrange("p (b n) -> p b n", n=128)
        Sout = NL[0:64, 3:5].rearrange("p l h n -> p (l h n)").rearrange("p (b n) -> p b n", n=128)
        Amf = scr[:, 3072:5120]
        Ams = Amf[0:NS, 0:512].rearrange("p (h k n) -> p h k n", h=4, k=4)
        UE = Amf[0:NS, 512:1536].rearrange("p (w b n) -> p w b n", w=2, b=DEC_B)
        ST = Amf[:, 1536:1600].rearrange("p (w n) -> p w n", w=2)
        lastc = wflat[:, 24 * NT - 100:24 * NT - 28].rearrange("p (c n) -> p c n", n=9)

        ffn_before = {s: sum(k == "ffn" for k, _ in stages[:s]) for s in range(len(stages) + 1)}


        shift_rows = W(SV_).rearrange("p c n -> p (c n)")[0:8, 0:D]
        shift_out = W(SV_).rearrange("p c n -> p (c n)")[0:9, D:2 * D]
        shift_cols = W(LORA_).rearrange("p c n -> p (c n)")[:, 5 * NT:5 * NT + 64].rearrange("p (c b) -> p c b", b=8)
        omka = hflat[:, 2272:2280]
        bank4h = bank[4][:, :].rearrange("p (h n) -> p h n", n=128)

        def pairs(i):
            return bank[i][:, :].rearrange("p (w h n) -> p w h n", w=2, h=2)

        blk64 = const("blk64")
        reset = const("reset")
        strict64, incl64 = const("strict64"), const("incl64")
        strict4, incl4 = const("strict4", NS), const("incl4", NS)
        seq4 = const("seq4", NS)
        vfirst_dram = nc.dram_tensor("v_first", (128, CH, NT), f32, kind="Internal").ap()

        shift_in = sem("shift_in")
        vfirst_in = sem("vfirst_in")
        shift_transposed = sem("shift_transposed")
        last_cols_ready = sem("last_cols_ready")
        last_rows_transposed = sem("last_rows_transposed")
        shift_out_ready = sem("shift_out_ready")
        shift_out_stored = sem("shift_out_stored")
        v_stored = sem("v_stored")
        xm_ready = sem("xm_ready")
        proj_evac = sem("proj_evac")
        cs_ready = sem("cs_ready")
        p_ready = sem("p_ready")
        cs_prev_ready = sem("cs_prev_ready")
        p_prev_ready = sem("p_prev_ready")
        kk_squared = sem("kk_squared")
        kk_ssq = sem("kk_ssq")
        kk_rms = sem("kk_rms")
        rk_ready = sem("rk_ready")
        rk_sum = sem("rk_sum")
        mixed_ready = sem("mixed_ready")
        tok_transposed = sem("tok_transposed")
        tok_ready_act = sem("tok_ready_act")
        tok_ready_dve = sem("tok_ready_dve")
        a_raw = sem("a_raw")
        a_masked = sem("a_masked")
        xt_start = sem("xt_start")
        nl_ready = sem("nl_ready")
        x0_raw = sem("x0_raw")
        x_ready = sem("x_ready")
        y_raw = sem("y_raw")
        y_ready = sem("y_ready")
        xy_raw = sem("xy_raw")
        rhs_raw = sem("rhs_raw")
        rhs_ready = sem("rhs_ready")
        u_raw = sem("u_raw")
        u_ready = sem("u_ready")
        ot_raw = sem("ot_raw")
        o_copied = sem("o_copied")
        t_ready = sem("t_ready")
        state_transposed = sem("state_transposed")
        state_out_ready = sem("state_out_ready")
        state_stored = sem("state_stored")
        s0_in = sem("s0_in")
        s0_transposed = sem("s0_transposed")
        t0_zeroed = sem("t0_zeroed")
        t0_ready = sem("t0_ready")
        st_raw = sem("st_raw")
        st_ready = sem("st_ready")
        ue_ready = sem("ue_ready")
        mean_raw = sem("mean_raw")
        centered = sem("centered")
        o_squared = sem("o_squared")
        var_raw = sem("var_raw")
        sd_ready = sem("sd_ready")
        og_ready = sem("og_ready")
        dve_step = sem("dve_step")
        act_step = sem("act_step")
        prompt_state_transposed = sem("prompt_state_transposed")
        state_out_ready_dve = sem("state_out_ready_dve")
        prompt_state_stored = sem("prompt_state_stored")
        so_raw = sem("so_raw")
        st_new_raw = sem("st_new_raw")


        def weight_piece(N, e):
            owner = max(s for s in unit_base if unit_base[s] <= N)
            k = 2 * CH if N - unit_base[owner] < GU_UNITS else FCH // 2
            return ring[:, N % SLOTS, 0:256 * k].rearrange("p (k c) -> p k c", c=256)[:, :, 128 * e:128 * e + 128], k

        def follow(eng):
            seen = {}

            def after(s_, n=1):
                seen[s_] = seen.get(s_, 0) + n
                eng.wait_ge(s_, seen[s_])
            return after

        def n_products(j):
            return 28 + 24 + (9 if j else 0)


        PRODUCTS = {"rwkv": lambda j: 52 + (9 if j else 0), "attn": lambda j: 24, "gdn": lambda j: 33, "ffn": lambda j: 0}
        proj_before = {}
        for s, (kind, n) in enumerate(stages):
            proj_before[s] = sum(PRODUCTS[k](i) for k, i in stages[:s])

        Q_, AO_ = 0, 3
        ATOK = wflat[:, 4 * CH * NT:4 * CH * NT + 6144].rearrange("p (w t n) -> p w t n", w=2, t=3)
        akey, aval = ATOK[:, 0], ATOK[:, 1]
        pages = wflat[:, 15360:23552].rearrange("p (w b g n) -> p w b g n", w=2, b=2, g=2)
        acon = wflat[:, 23552:23552 + ATTN_ARRAY.shape[1]]
        pageT = wflat[:, 25600:27648].rearrange("p (h g n) -> p h g n", h=8, g=2)
        scrA = wflat[:, 25600:27648]
        prob = scrA[:, 0:1024].rearrange("p (a w n) -> p a w n", a=2, w=2)
        pdiff = scrA[:, 1024:1536].rearrange("p (a n) -> p a n", a=2)
        probT = scrA[:, 1536:2048].rearrange("p (a k n) -> p a k n", a=2, k=2)
        fbias = scrA[0:AH, 0:FN]
        lamw = W(AO_).rearrange("p c n -> p (c n)")[:, 0:256].rearrange("p (a n) -> p a n", a=4)
        rel_ext = W(AO_).rearrange("p c n -> p (c n)")[0:BUCKETS + 1, 256:264]
        rel_rows = W(AO_).rearrange("p c n -> p (c n)")[0:BUCKETS + 1, 512:1024].rearrange("p (i r) -> p i r", i=DEC_T)
        hankel = hflat[:, 0:2048].rearrange("p (h n) -> p h n", h=8)
        q_split = hflat[:, 0:512].rearrange("p (b h n) -> p b h n", b=8, h=8)
        scoreT = hflat[:, 512:768].rearrange("p (g r) -> p g r", g=2)
        scoreNT = hflat[0:NS, 768:896]
        sprob = hflat[:, 896:896 + SK]
        sprobT = hflat[:, 1184:1568].rearrange("p (g r) -> p g r", g=3)
        sdiffT = hflat[:, 1568:1760].rearrange("p (g r) -> p g r", g=3)
        sbias = rms
        acol = sb("acol", [128, 32])
        neg_max, expsum, rcp, coef = (acol[:, 4 * i:4 * i + 4] for i in range(4))
        lam_col, sub_col, half_coef = acol[:, 16:17], acol[:, 17:18], acol[:, 18:19]
        lam_tmp = acol[:, 20:24]
        page_ids = sb("page_ids", [1, 16], mybir.dt.int32)
        bias_dram = nc.dram_tensor("bias_by_distance", (AH, FN), f32, kind="Internal").ap()

        def acon_at(name, p=128):
            a, b = ATTN_COLS[name]
            return acon[0:p, a:b]

        attn_in = sem("attn_in")
        lam_sums = cs_ready
        lam_exp = p_prev_ready
        rel_const = sem("rel_const")
        fb_raw = st_raw
        fb_ready = sem("fb_ready")
        fb_stored = sem("fb_stored")
        hankel_in = sem("hankel_in")
        sbias_raw = sem("sbias_raw")
        sbias_ready = sem("sbias_ready")
        rel_rows_ready = last_cols_ready
        ktok_raw = sem("ktok_raw")
        vtok_raw = sem("vtok_raw")
        ktok_ready = sem("ktok_ready")
        vtok_ready = sem("vtok_ready")
        kv_stored = sem("kv_stored")
        score_raw = a_raw
        max_ready = cs_prev_ready
        exp_ready = sem("exp_ready")
        diff_ready = sem("diff_ready")
        probT_raw = sem("probT_raw")
        probT_ready = sem("probT_ready")
        ao_raw = st_new_raw
        ao_ready = sem("ao_ready")
        page_ids_in = sem("page_ids_in")
        kpage_in = [sem(f"kpage_in{e}") for e in range(2)]
        vpage_in = sem("vpage_in")
        q_split_ready = mixed_ready
        pageT_raw = sem("pageT_raw")
        pageT_ready_act = sem("pageT_ready_act")
        pageT_ready_dve = sem("pageT_ready_dve")
        sT_raw = sem("sT_raw")
        sT_ready = rhs_ready
        s_raw = mean_raw
        s_biased = centered
        s_exp = p_ready
        sprob_ready = sem("sprob_ready")
        sprobT_raw = sem("sprobT_raw")
        sprobT_ready = sem("sprobT_ready")
        sdiff_ready = ue_ready
        so2_raw = sem("so2_raw")
        sub_squared = sem("sub_squared")
        sub_ssq = kk_ssq
        sub_rms = sem("sub_rms")

        GZ_, GO_ = 3, 4
        gs = wflat[:, 5 * CH * NT:12 * CH * NT]

        def cut(at, shape):
            n = int(np.prod(shape))
            names = "abcd"[:len(shape)]
            ap = gs[:, at:at + n]
            if len(shape) == 1:
                return ap
            return ap.rearrange(f"p ({' '.join(names)}) -> p {' '.join(names)}", **dict(zip(names[1:], shape[1:])))

        XP = SEQ + 3 + 7 * DEC_B
        xp = cut(0, (4, XP))
        conv_prev = cut(1260, (24, 24))
        conv_rows = cut(1836, (3072,))[0:24]
        tails = cut(4908, (24, 27))
        tail_rows = cut(5556, (3072,))[0:27]
        ctmp = cut(8628, (2, NT))
        gtokV, gtokK = cut(0, (1024,)), cut(1024, (1024,))
        aqk, gN = cut(2048, (4, 128)), cut(2560, (4, 128))
        gNL = cut(3072, (6, 4, 128))
        gX, gXT, gY = cut(6144, (4, 128)), cut(6656, (4, 128)), cut(7168, (4, 128))
        gXboth = cut(6144, (2, 4, 128))
        gE, gG = cut(7680, (4, 128)), cut(8192, (4, 128))
        gR, gU, gUd, gOt = (cut(8704 + 512 * i, (4, 128)) for i in range(4))
        gS = cut(10752, (8, 128))
        gS0 = cut(11776, (2, 8, 128))
        gUe = cut(13824, (8, 128))
        gST = cut(14848, (2, NS))
        gsq = cut(0, (CH, NT))
        gsd = cut(2304, (CH, NT))
        graw = cut(14912, (3, 16))
        gcol = cut(14960, (8, 3, 8))
        BETA, G_, EGC, NEGC, EDL, EGL, BEDL, NBETA = range(8)
        gtmp = cut(15152, (2, 3, 8))
        gpar = cut(15200, (2, 8))
        gGb = cut(15216, (8, 8))
        egLs = cut(15280, (8, 8))

        conv_in = shift_in
        gpar_in = sem("gpar_in")
        prev_raw = shift_transposed
        prev_ready = sem("prev_ready")
        pads_zeroed = sem("pads_zeroed")
        xp_ready = sem("xp_ready")
        conv_done = sem("conv_done")
        tail_done = sem("tail_done")
        tails_raw = last_rows_transposed
        tail_rows_ready = sem("tail_rows_ready")
        conv_stored = sem("conv_stored")
        qkv_silu = sem("qkv_silu")
        qk_squared = kk_squared
        qk_ssq = sem("qk_ssq")
        qk_rms = sem("qk_rms")
        qk_ready = sem("qk_ready")
        g_abs = cs_ready
        g_ln = p_ready
        g_ready = mixed_ready
        gsum_raw = rk_sum
        gsum_ready = sem("gsum_ready")
        gexp_ready = sem("gexp_ready")
        g_spread = last_cols_ready
        dec_raw = sprobT_raw
        gram_raw = a_raw
        dec_ready = p_prev_ready
        gn_masked = sem("gn_masked")
        gtok_raw = sbias_raw
        gtok_ready = sem("gtok_ready")
        ks_raw = mean_raw
        r_ready = sem("r_ready")
        w_raw = rhs_raw
        gu_ready = rhs_ready
        go1_raw = sT_raw
        go1_ready = sprobT_ready
        go2_raw = so_raw
        gs_raw = st_new_raw
        gs_ready = sem("gs_ready")
        gs_zeroed = sem("gs_zeroed")
        got_ready = tok_ready_dve
        goT_raw = var_raw
        goT_ready = sem("goT_ready")
        gstate_in = [sem(f"gstate{i}_in") for i in range(2)]
        gst_raw = st_raw
        gst_ready = st_ready
        gue_ready = ue_ready
        gstate_stored = [sem(f"gstate{i}_stored") for i in range(2)]
        gstate_p_stored = sem("gstate_p_stored")

        row_loads = []
        at = 0
        while at < NROWS:
            src, i0 = rows[at]
            k, p0 = divmod(at, 128)
            n = 1
            while at + n < NROWS and rows[at + n][0] is src and p0 + n < 128:
                n += 1
            row_loads.append((src, i0, k, p0, n))
            at += n
        N_CONST_LOADS = 1 + len(row_loads)

        block = ctx.enter_context(nc.Block())

        @block.sync
        def _(sp):
            wg = t["ffn_w_gate"].rearrange("l a (k q) n -> (l a) q k n", q=128)
            wu = t["ffn_w_up"].rearrange("l a (k q) n -> (l a) q k n", q=128)
            wd = t["ffn_w_down"].rearrange("l a (k q) n -> (l a) q k n", q=128)

            def gate_up_unit(n, slot, col, free):
                sp.wait_ge(w_lo_ready, free)
                dst = ring[:, slot, :].rearrange("p (w k c) -> p w k c", w=2, c=256)
                sp.dma_start(dst[:, 0], wg[n, :, :, bass.ds(col, 256)]).then_inc(slot_full[slot], 16)
                sp.dma_start(dst[:, 1], wu[n, :, :, bass.ds(col, 256)]).then_inc(slot_full[slot], 16)

            def down_unit(n, slot, half, col, free):
                sp.wait_ge(w_lo_ready, free)
                dst = ring[:, slot, 0:11 * 256].rearrange("p (k c) -> p k c", c=256)
                k0 = 11 * half
                sp.dma_start(dst[:, 0:6], wd[n, :, k0:k0 + 6, bass.ds(col, 256)]).then_inc(slot_full[slot], 16)
                sp.dma_start(dst[:, 6:11], wd[n, :, k0 + 6:k0 + 11, bass.ds(col, 256)]).then_inc(slot_full[slot], 16)

            def wait_released(N):
                if N < 0:
                    return
                owner = max(s for s in unit_base if unit_base[s] <= N)
                if stages[owner][0] == "ffn":
                    sp.wait_ge(w_lo_ready, split_credit(owner) + 2 * (N - unit_base[owner] + 1))
                else:
                    sp.wait_ge(half_done, released(N))

            def list_unit(N):
                wait_released(N - SLOTS)
                for off, p, k, n, src in units[N][0]:
                    dst = ring[0:p, N % SLOTS, off:off + k * n].rearrange("p (k n) -> p k n", n=n)
                    sp.dma_start(dst, src).then_inc(slot_full[N % SLOTS], 16)

            for s, (kind, n) in enumerate(stages):
                b = unit_base[s]
                if kind != "ffn":
                    for N in range(b, unit_base.get(s + 1, len(units))):
                        list_unit(N)
                if kind == "ffn":
                    free = lambda u: split_credit(s) + 2 * (u - SLOTS + 1)
                    for j in range(SLOTS):
                        if s and stages[s - 1][0] != "ffn":
                            wait_released(b + j - SLOTS)
                        gate_up_unit(n, (b + j) % SLOTS, j * 256, free(j))
                    for j in range(4, 11):
                        gate_up_unit(n, (b + j) % SLOTS, j * 256, free(j))
                    with sp.Fori(0, 2) as i:
                        for j in range(4):
                            down_unit(n, (b + 11 + j) % SLOTS, j % 2, i * 512 + (j // 2) * 256, i * 8 + free(11 + j))

        @block.tensor
        def _(pe):
            pe.sem_inc(half_done, 2 * SLOTS)
            pe.wait_ge(consts_in, N_CONST_LOADS * 16)
            pe.wait_ge(consts_set, 1)
            for k, n in ROW_TILES:
                last = nc.tensor.transpose(bank[0][:, 128 * k:128 * k + n], prm_rows[0:n, k, :], ident[0:n, 0:n])
            last.then_inc(prm_transposed, 1)
            pe.wait_ge(x_in, 48)
            for c in range(CH):
                if c >= 4:
                    pe.wait_ge(x_updated, c - 3)
                for i, (t0, tn) in enumerate(TOK_TILES):
                    last = nc.tensor.transpose(bank[4 + c % 4][:, t0:t0 + tn], xin[0:tn, i, 128 * c:128 * c + 128],
                                               ident[0:tn, 0:tn])
                last.then_inc(x_transposed, 1)

            def norm(k):
                for c in range(CH):
                    pe.wait_ge(squared, 8 * k + c + 1)
                    last = nc.tensor.matmul(bank[0][:, 0:NT], ones[:, :], h[:, c, :], start=(c == 0), stop=(c == CH - 1))
                last.then_inc(ssq_done, 1)

            def three_products(out, w_hi_k, w_lo_k, x_hi_k, x_lo_k, start, stop):
                nc.tensor.matmul(out, w_hi_k, x_hi_k, start=start, stop=False)
                nc.tensor.matmul(out, w_lo_k, x_hi_k, start=False, stop=False)
                return nc.tensor.matmul(out, w_hi_k, x_lo_k, start=False, stop=stop)

            def gate_up_unit(w_ready, free, parts=None):
                for e in range(2):
                    pe.wait_ge(w_lo_ready, w_ready + e)
                    pe.wait_ge(gate_up_free, free + e)
                    for side in range(2):
                        for k in range(CH):
                            if parts is not None and e == 0 and side == 0:
                                pe.wait_ge(act_lo_ready, parts + k + 1)
                            last = three_products(bank[2 * e + side][:, 0:NT], w_hi[e][:, 8 * side + k, :],
                                                  w_lo[e][:, 8 * side + k, :], h_hi[:, k, :], h_lo[:, k, :],
                                                  k == 0, k == CH - 1)
                    last.then_inc(half_done, 1)

            after = follow(pe)

            def unit_in(N):
                pe.wait_ge(slot_full[N % SLOTS], full(N))

            def square(N, src, d0, banks_free):
                for d in range(8):
                    if d % 4 == 0:
                        unit_in(N + d // 4)
                    banks_free(d)
                    w = ring[:, (N + d // 4) % SLOTS, :].rearrange("p (k n) -> p k n", n=512)
                    for k in range(CH):
                        last = nc.tensor.matmul(bank[(d0 + d) % 8][:, 0:NT], w[:, k, 128 * (d % 4):128 * (d % 4) + 128],
                                                src[:, k, :], start=(k == 0), stop=(k == CH - 1))
                    if d % 2:
                        last.then_inc(half_done, 1)

            def rwkv(s, j):
                b = unit_base[s]
                base = proj_before[s]
                after(shift_in, 16)
                for c in range(CH):
                    last = nc.tensor.transpose(bank[7][:, 8 * c:8 * c + 8], shift_rows[:, 128 * c:128 * c + 128], ident[0:8, 0:8])
                last.then_inc(shift_transposed, 1)
                after(last_cols_ready)
                for c in range(CH):
                    last = nc.tensor.transpose(bank[6 - c // 4][0:9, 128 * (c % 4):128 * (c % 4) + 128], lastc[:, c, :], ident)
                last.then_inc(last_rows_transposed, 1)

                p = 0

                def free():
                    if p >= 8:
                        pe.wait_ge(proj_evac, base + p - 7)

                unit_in(b)
                wa = ring[:, b % SLOTS, :]
                hidden = [(0, 64, 0, 64), (512, 64, 0, 64), (1024, 160, 0, 128), (1024, 160, 128, 32)]
                if j:
                    hidden.append((2304, 32, 0, 32))
                for i, (off, width, c0, cn) in enumerate(hidden):
                    if i != 3:
                        after(xm_ready)
                    src = W((XM0_, XM1_, XM0_, XM0_, XM1_)[i])
                    w = wa[:, off:off + 8 * width].rearrange("p (k n) -> p k n", n=width)
                    for k in range(CH):
                        last = nc.tensor.matmul(bank[p % 8][0:cn, 0:NT], w[:, k, c0:c0 + cn], src[:, k, :],
                                                start=(k == 0), stop=(k == CH - 1))
                    last.then_inc(half_done, 1)
                    p += 1
                if not j:
                    after(xm_ready)
                unit_in(b + 1)
                wb = ring[:, (b + 1) % SLOTS, :]
                outs = [(wb, 0, 64, 0, None), (wb, 1024, 64, 1, None), (wb, 2048, 128, 2, (3072, 32, 3))]
                if j:
                    outs.append((wa, 2560, 32, 4, None))
                for w, off, kn, hrow, more in outs:
                    pe.wait_ge(proj_evac, base + (hrow if more is None else 3) + 1)
                    for d in range(8):
                        free()
                        last = nc.tensor.matmul(bank[p % 8][:, 0:NT], w[0:kn, off + 128 * d:off + 128 * d + 128],
                                                lora_h[0:kn, hrow, :], start=True, stop=more is None)
                        if more:
                            off2, kn2, hrow2 = more
                            last = nc.tensor.matmul(bank[p % 8][:, 0:NT], w[0:kn2, off2 + 128 * d:off2 + 128 * d + 128],
                                                    lora_h[0:kn2, hrow2, :], start=False, stop=True)
                        last.then_inc(half_done, 1)
                        p += 1
                for i in range(3):
                    if i:
                        after(xm_ready)
                    p0 = p
                    square(b + 2 + 2 * i, W((XM1_, XM0_, XM1_)[i]), p0,
                           lambda d: pe.wait_ge(proj_evac, base + p0 + d - 7))
                    p += 8

                after(kk_squared)
                pe.wait_ge(proj_evac, base + p)
                for c in range(CH):
                    nc.tensor.matmul(bank[c][:, 0:NT], blk64, W(LORA_)[:, c, :], start=True, stop=True).then_inc(kk_ssq, 1)
                after(rk_ready)
                for c in range(CH):
                    after(kk_rms)
                    nc.tensor.matmul(bank[c][:, 0:NT], blk64, W(BONUS_)[:, c, :], start=True, stop=True).then_inc(rk_sum, 1)
                after(mixed_ready)

                for tile, (t0, tn) in enumerate(TOK_TILES):
                    for a, (src, dst) in enumerate(((V_, tokV), (BT_, tokB), (KT_, tokK))):
                        for c in range(CH):
                            last = nc.tensor.transpose(bank[2 * a + c // 4][0:tn, 128 * (c % 4):128 * (c % 4) + 128],
                                                       W(src)[:, c, t0:t0 + tn], ident)
                        last.then_inc(tok_transposed, 1)
                    after(tok_ready_act, 2)
                    after(tok_ready_dve)
                    levels = 6 if tile < 2 else 2
                    am = Am if tile < 2 else Ams
                    for g in range(4):
                        for i in range(4):
                            hp, r0 = 2 * g + i // 2, 64 * (i % 2)
                            for kd, (l, r) in enumerate(((BT_, AT_), (KT_, AT_), (BT_, RT_), (KT_, RT_))):
                                last = nc.tensor.matmul(bank[i][0:tn, 128 * kd:128 * kd + tn],
                                                        W(l)[r0:r0 + 64, hp, t0:t0 + tn],
                                                        W(r)[r0:r0 + 64, hp, t0:t0 + tn], start=True, stop=True)
                            last.then_inc(a_raw, 1)
                        ladder(tn, levels, NL, Xm, XT, Ym)
                        if tile < 2:
                            chunk_states(g, t0)
                        else:
                            for e in range(2):
                                sample_states(g, e)
                    if tile == 1:
                        for c in range(CH):
                            last = nc.tensor.transpose(bank[c // 4][:, 128 * (c % 4):128 * (c % 4) + 128], Tbd[:, c, :], ident)
                        last.then_inc(prompt_state_transposed, 1)
                        after(t0_zeroed)

                for c in range(CH):
                    nc.tensor.matmul(bank[c][:, 0:NT], blk64, W(O_)[:, c, :], start=True, stop=True).then_inc(mean_raw, 1)
                for c in range(CH):
                    after(o_squared)
                    nc.tensor.matmul(bank[c][:, 0:NT], blk64, W(PI_)[:, c, :], start=True, stop=True).then_inc(var_raw, 1)
                after(sd_ready, 8)
                after(og_ready, 8)
                square(b + 8, W(O_), 0, lambda d: None)

            def ladder(tn, levels, NL, Xm, XT, Ym):
                after(xt_start)
                for e in range(2):
                    for q in range(2):
                        last = nc.tensor.transpose(bank[(4, 7)[e]][0:tn, 128 * q:128 * q + tn], XT[0:tn, 2 * e + q, 0:tn],
                                                   ident[0:tn, 0:tn])
                    last.then_inc(x0_raw, 1)
                for l in range(1, levels):
                    after(nl_ready)
                    for e in range(2):
                        after(x_ready)
                        for q in range(2):
                            i = 2 * e + q
                            last = nc.tensor.matmul(bank[(4, 7)[e]][0:tn, 128 * q:128 * q + tn], NL[0:tn, l - 1, i, 0:tn],
                                                    Xm[0:tn, i, 0:tn], start=True, stop=True)
                        last.then_inc(y_raw, 1)
                    for e in range(2):
                        after(y_ready)
                        for q in range(2):
                            i = 2 * e + q
                            if l < levels - 1:
                                nc.tensor.matmul(bank[5 + e][0:tn, 128 * q:128 * q + tn], XT[0:tn, i, 0:tn], Ym[0:tn, i, 0:tn],
                                                 start=True, stop=True)
                            last = nc.tensor.matmul(bank[5 + e][0:tn, 256 + 128 * q:256 + 128 * q + tn], Ym[0:tn, i, 0:tn],
                                                    XT[0:tn, i, 0:tn], start=True, stop=True)
                        last.then_inc(xy_raw, 1)
                after(x_ready, 2)

            def chunk_states(g, t0):
                for ch in range(2):
                    r = slice(64 * ch, 64 * ch + 64)
                    t = slice(t0 + 64 * ch, t0 + 64 * ch + 64)
                    for e in range(2):
                        hp = 2 * g + e
                        nc.tensor.matmul(bank[7][r, 128 * e:128 * e + 128], W(AT_)[:, hp, t], Tbd[:, hp, :],
                                         start=True, stop=False, skip_group_check=True)
                        for q in range(2):
                            i = 2 * e + q
                            last = nc.tensor.matmul(bank[7][r, 64 * i:64 * i + 64], Am[:, i, 1, r],
                                                    tokV[:, 256 * g + 64 * i:256 * g + 64 * i + 64],
                                                    start=False, stop=(q == 1), skip_group_check=True)
                    last.then_inc(rhs_raw, 1)
                    after(rhs_ready)
                    for i in range(GROUP):
                        last = nc.tensor.matmul(bank[7][r, 256 + 64 * i:256 + 64 * i + 64], XT[:, i, r], Rhs[:, 64 * i:64 * i + 64],
                                                start=True, stop=True)
                    last.then_inc(u_raw, 1)
                    after(u_ready)
                    for e in range(2):
                        hp = 2 * g + e
                        o = slice(128 * e + 64 * ch, 128 * e + 64 * ch + 64)
                        nc.tensor.matmul(bank[4][:, o], Tbd[:, hp, :], W(RT_)[:, hp, t], start=True, stop=False,
                                         skip_group_check=True)
                        for q in range(2):
                            i = 2 * e + q
                            out = bank[4][64 * q:64 * q + 64, o]
                            nc.tensor.matmul(out, Um[:, 64 * i:64 * i + 64], Am[:, i, 2, r], start=False, stop=False,
                                             skip_group_check=True)
                            nc.tensor.matmul(out, tokV[:, 256 * g + 64 * i:256 * g + 64 * i + 64], Am[:, i, 3, r],
                                             start=False, stop=True, skip_group_check=True)
                    for e in range(2):
                        hp = 2 * g + e
                        out = bank[5][:, 128 * e:128 * e + 128]
                        nc.tensor.matmul(out, tokB[r, 128 * hp:128 * hp + 128], Um[r, 128 * e:128 * e + 128], start=True, stop=False)
                        last = nc.tensor.matmul(out, tokK[r, 128 * hp:128 * hp + 128], tokV[r, 128 * hp:128 * hp + 128],
                                                start=False, stop=True)
                    last.then_inc(ot_raw, 1)
                    after(o_copied)
                    after(t_ready)

            def sample_states(g, e):
                hp = 2 * g + e
                after(s0_in, 32)
                for b in range(DEC_B):
                    last = nc.tensor.transpose(bank[0][:, 64 * b:64 * b + 64], S0[:, b, :], ident[0:64, 0:64])
                last.then_inc(s0_transposed, 1)
                after(t0_ready)
                for b in range(DEC_B):
                    c0 = SEQ + DEC_T * b
                    last = nc.tensor.matmul(bank[1][:, 8 * b:8 * b + 8], Tbd[:, b, :],
                                            work[:, RT_:AT_ + 1:AT_ - RT_, hp, c0:c0 + DEC_T], start=True, stop=True)
                last.then_inc(st_raw, 1)
                after(st_ready)
                nc.tensor.matmul(bank[2][0:NS, 0:128], ST[:, 1, :], ident, start=True, stop=False, skip_group_check=True)
                for q in range(2):
                    i = 2 * e + q
                    last = nc.tensor.matmul(bank[2][0:NS, 64 * q:64 * q + 64], Ams[:, i, 1, :],
                                            tokV[0:NS, 128 * hp + 64 * q:128 * hp + 64 * q + 64], start=False, stop=True,
                                            skip_group_check=True)
                last.then_inc(rhs_raw, 1)
                after(rhs_ready)
                for q in range(2):
                    last = nc.tensor.matmul(bank[2][0:NS, 128 + 64 * q:128 + 64 * q + 64], XT[0:NS, 2 * e + q, 0:NS],
                                            Rhs[0:NS, 64 * q:64 * q + 64], start=True, stop=True)
                last.then_inc(u_raw, 1)
                after(u_ready)
                for q in range(2):
                    i = 2 * e + q
                    out = bank[3][64 * q:64 * q + 64, 0:NS]
                    nc.tensor.matmul(out, Um[0:NS, 64 * q:64 * q + 64], Ams[:, i, 2, :], start=True, stop=False)
                    last = nc.tensor.matmul(out, tokV[0:NS, 128 * hp + 64 * q:128 * hp + 64 * q + 64], Ams[:, i, 3, :],
                                            start=False, stop=True)
                last.then_inc(so_raw, 1)
                for q in range(2):
                    after(ue_ready)
                    out = bank[4][64 * q:64 * q + 64, :]
                    c = slice(128 * hp + 64 * q, 128 * hp + 64 * q + 64)
                    nc.tensor.matmul(out, tokB[0:NS, c], UE[:, 0, :, :].rearrange("p b n -> p (b n)"), start=True, stop=False)
                    last = nc.tensor.matmul(out, tokK[0:NS, c], UE[:, 1, :, :].rearrange("p b n -> p (b n)"), start=False, stop=True)
                    last.then_inc(st_new_raw, 1)
                after(t_ready)
                for b in range(DEC_B):
                    last = nc.tensor.transpose(bank[5 + b // 4][0:64, 128 * (b % 4):128 * (b % 4) + 128], Tst[:, b, :], ident)
                last.then_inc(state_transposed, 1)
                after(state_out_ready, 2)

            def attention(s):
                b = unit_base[s]
                base = proj_before[s]
                pe.wait_ge(h_ready, 8 * (s + 1))
                for i in range(3):
                    square(b + 2 * i, h, 8 * i, lambda d: pe.wait_ge(proj_evac, base + 8 * i + d - 7) if i else None)
                pe.wait_ge(proj_evac, base + 24)
                after(attn_in, 16 * 3)
                after(rel_const)
                nc.tensor.matmul(bank[0][0:AH, 0:FN], rel_ext, acon_at("by_distance", BUCKETS + 1), start=True, stop=True).then_inc(fb_raw, 1)
                after(rel_rows_ready)
                for i in range(DEC_T):
                    last = nc.tensor.matmul(bank[1][:, 0:SK], rel_rows[:, i, :], acon_at(f"sample{i}", BUCKETS + 1),
                                            start=(i == 0), stop=(i == DEC_T - 1))
                last.then_inc(sbias_raw, 1)
                for i, (t0, tn) in enumerate(TOK_TILES):
                    for w, (src, raw, ready) in enumerate(((1, ktok_raw, ktok_ready), (2, vtok_raw, vtok_ready))):
                        if i:
                            after(ready)
                        for c in range(CH):
                            last = nc.tensor.transpose(bank[2 + 2 * w + c // 4][0:tn, 128 * (c % 4):128 * (c % 4) + 128],
                                                       W(src)[:, c, t0:t0 + tn], ident)
                        last.then_inc(raw, 1)
                after(ktok_ready)
                after(vtok_ready)
                after(sbias_ready)
                after(hankel_in, 16)
                jobs = [(hd, qt) for hd in range(AH) for qt in range(2)]

                def scores(n):
                    hd, qt = jobs[n]
                    nk = 128 * (qt + 1)
                    for sub in range(2):
                        r = slice(64 * sub, 64 * sub + 64)
                        out = bank[2 * (n % 2) + sub][:, 0:nk]
                        nc.tensor.matmul(out, W(Q_)[r, hd, 128 * qt:128 * qt + 128], W(1)[r, hd, 0:nk], start=True, stop=False)
                        last = nc.tensor.matmul(out, acon_at("flip"), hankel[:, hd, 128 - 128 * qt:128 - 128 * qt + nk], start=False, stop=True)
                    last.then_inc(score_raw, 1)

                def transpose_probs(n):
                    after(diff_ready)
                    for k in range(jobs[n][1] + 1):
                        last = nc.tensor.transpose(bank[4 + n % 2][:, 128 * k:128 * k + 128], pdiff[:, n % 2, 128 * k:128 * k + 128], ident)
                    last.then_inc(probT_raw, 1)

                def values(n):
                    hd, qt = jobs[n]
                    after(probT_ready)
                    if n >= 2:
                        after(ao_ready)
                    for k in range(qt + 1):
                        last = nc.tensor.matmul(bank[6 + n % 2][:, 0:128], aval[:, k, 128 * hd:128 * hd + 128], probT[:, n % 2, k, :],
                                                start=(k == 0), stop=(k == qt))
                    last.then_inc(ao_raw, 1)

                for n in range(len(jobs) + 2):
                    if n < len(jobs):
                        if n >= 2:
                            pe.wait_ge(exp_ready, n - 1)
                        scores(n)
                    if 1 <= n <= len(jobs):
                        transpose_probs(n - 1)
                    if n >= 2:
                        values(n - 2)
                after(ao_ready, 2)

                after(q_split_ready)
                for r in range(4):
                    for e in range(2):
                        b_ = 2 * r + e
                        after(kpage_in[e], 32)
                        for hd in range(AH):
                            for g in range(2):
                                last = nc.tensor.transpose(bank[hd // 2][:, 256 * (hd % 2) + 128 * g:256 * (hd % 2) + 128 * g + 128],
                                                           pages[:, 0, e, g, 128 * hd:128 * hd + 128], ident)
                            if hd % 4 == 3:
                                last.then_inc(pageT_raw, 1)
                        after(pageT_ready_act)
                        after(pageT_ready_dve)
                        for hd in range(AH):
                            for g in range(2):
                                nc.tensor.matmul(bank[4][:, 64 * g + 8 * hd:64 * g + 8 * hd + 8], pageT[:, hd, g, :],
                                                 q_split[:, b_, hd, :], start=True, stop=True)
                            last = nc.tensor.matmul(bank[5][0:NS, 8 * hd:8 * hd + 8], W(1)[:, hd, SEQ:], q_split[:, b_, hd, :],
                                                    start=True, stop=True)
                        last.then_inc(sT_raw, 1)
                        after(sT_ready)
                    for g in range(2):
                        nc.tensor.transpose(bank[6][:, 128 * g:128 * g + 128], scoreT[:, g, :], ident)
                    nc.tensor.transpose(bank[6][:, 256:SK], scoreNT, ident[0:NS, 0:NS]).then_inc(s_raw, 1)
                    after(sprob_ready)
                    for g in range(2):
                        nc.tensor.transpose(bank[0][:, 128 * g:128 * g + 128], sprob[:, 128 * g:128 * g + 128], ident)
                    nc.tensor.transpose(bank[0][0:NS, 256:384], sprob[:, 256:SK], ident).then_inc(sprobT_raw, 1)
                    after(sdiff_ready)
                    after(vpage_in, 64)
                    for e in range(2):
                        for hd in range(AH):
                            out = bank[7][:, 32 * e + 4 * hd:32 * e + 4 * hd + 4]
                            cols = slice(32 * e + 4 * hd, 32 * e + 4 * hd + 4)
                            for g in range(2):
                                nc.tensor.matmul(out, pages[:, 1, e, g, 128 * hd:128 * hd + 128], sdiffT[:, g, cols],
                                                 start=(g == 0), stop=False)
                            last = nc.tensor.matmul(out, aval[0:NS, 2, 128 * hd:128 * hd + 128], sdiffT[0:NS, 2, cols],
                                                    start=False, stop=True)
                    last.then_inc(so2_raw, 1)
                    after(ao_ready)
                for c in range(CH):
                    after(sub_squared)
                    nc.tensor.matmul(bank[c][:, 0:NT], ones, W(Q_)[:, c, :], start=True, stop=True).then_inc(sub_ssq, 1)
                after(sub_rms, 8)
                after(og_ready, 8)
                square(b + 6, W(AO_), 0, lambda d: None)

            def gdn(s):
                b = unit_base[s]
                base = proj_before[s]
                pe.wait_ge(h_ready, 8 * (s + 1))
                after(conv_in, 16)
                for c in range(24):
                    last = nc.tensor.transpose(bank[6 + c // 12][:, 24 * (c % 12):24 * (c % 12) + 24],
                                               conv_rows[:, 128 * c:128 * c + 128], ident[0:24, 0:24])
                last.then_inc(prev_raw, 1)
                unit_in(b)
                w = ring[:, b % SLOTS, 0:128].rearrange("p (k n) -> p k n", n=16)
                for i, (t0, tn) in enumerate(TOK_TILES):
                    for k in range(CH):
                        last = nc.tensor.matmul(bank[0][0:tn, 16 * i:16 * i + 16], h[:, k, t0:t0 + tn], w[:, k, :],
                                                start=(k == 0), stop=(k == CH - 1))
                last.then_inc(half_done, 1)
                after(prev_ready)
                for i in range(4):
                    square(b + 1 + 2 * i, h, 8 * i + 1,
                           lambda d: pe.wait_ge(proj_evac, base + 8 * i + d - 6) if 8 * i + d >= 7 else None)
                pe.wait_ge(proj_evac, base + 33)
                after(tail_done, 24)
                for c in range(24):
                    last = nc.tensor.transpose(bank[c // 4][0:27, 128 * (c % 4):128 * (c % 4) + 128], tails[:, c, :], ident)
                last.then_inc(tails_raw, 1)
                after(tail_rows_ready)
                for i in range(2):
                    for c in range(CH):
                        after(qk_squared)
                        if i:
                            after(qk_rms)
                        nc.tensor.matmul(bank[c][:, 0:NT], ones, gsq[:, c, :], start=True, stop=True).then_inc(qk_ssq, 1)
                after(qk_rms, 8)
                after(qk_ready)
                after(g_ready)
                for i, (t0, tn) in enumerate(TOK_TILES):
                    incl, same = (const("incl128"), ones) if i < 2 else (const("incl4", NS), const("same4", NS))
                    nc.tensor.matmul(bank[0][0:tn, 8 * i:8 * i + 8], incl, gcol[0:tn, G_, i, :], start=True, stop=True)
                    nc.tensor.matmul(bank[0][0:tn, 32 + 8 * i:40 + 8 * i], same, gcol[0:tn, G_, i, :], start=True, stop=True)
                nc.tensor.matmul(bank[0][:, 64:128], ones[0:NS, :], gGb[0:NS].rearrange("p b h -> p (b h)"), start=True, stop=True).then_inc(gsum_raw, 1)
                after(gsum_ready)
                after(gexp_ready)
                after(gs_zeroed)
                for tile, (t0, tn) in enumerate(TOK_TILES):
                    for a, src in enumerate((2, 1)):
                        for c in range(CH):
                            last = nc.tensor.transpose(bank[2 * a + c // 4][0:tn, 128 * (c % 4):128 * (c % 4) + 128],
                                                       W(src)[:, c, t0:t0 + tn], ident)
                        last.then_inc(gtok_raw, 1)
                    after(gtok_ready, 2)
                    levels = 7 if tile < 2 else 2
                    incl = const("incl128") if tile < 2 else const("incl4", NS)
                    tk = slice(t0, t0 + tn)
                    for g in range(2):
                        after(g_spread)
                        for i in range(GROUP):
                            last = nc.tensor.matmul(bank[0][0:tn, 128 * i:128 * i + tn], gG[0:tn, i, 0:tn], incl, start=True, stop=True)
                        last.then_inc(dec_raw, 1)
                        for i in range(GROUP):
                            hd = 4 * g + i
                            nc.tensor.matmul(bank[1][0:tn, 128 * i:128 * i + tn], W(1)[:, hd, tk], W(1)[:, hd, tk], start=True, stop=True)
                            last = nc.tensor.matmul(bank[2][0:tn, 128 * i:128 * i + tn], W(1)[:, hd, tk], W(0)[:, hd, tk], start=True, stop=True)
                        last.then_inc(gram_raw, 1)
                        ladder(tn, levels, gNL, gX, gXT, gY)
                        if tile < 2:
                            for i in range(GROUP):
                                hd = 4 * g + i
                                last = nc.tensor.matmul(bank[7][:, 128 * i:128 * i + 128], W(1)[:, hd, tk], gS[:, hd, :], start=True, stop=True)
                            last.then_inc(ks_raw, 1)
                            for i in range(GROUP):
                                hd = 4 * g + i
                                last = nc.tensor.matmul(bank[4][:, 128 * i:128 * i + 128], W(0)[:, hd, tk], gS[:, hd, :], start=True, stop=True)
                            last.then_inc(go1_raw, 1)
                            after(r_ready)
                            for i in range(GROUP):
                                last = nc.tensor.matmul(bank[5][:, 128 * i:128 * i + 128], gXT[:, i, :], gR[:, i, :], start=True, stop=True)
                            last.then_inc(w_raw, 1)
                            after(gu_ready)
                            for i in range(GROUP):
                                last = nc.tensor.matmul(bank[6][:, 128 * i:128 * i + 128], aqk[:, i, :], gU[:, i, :], start=True, stop=True)
                            last.then_inc(go2_raw, 1)
                            for i in range(GROUP):
                                hd = 4 * g + i
                                last = nc.tensor.matmul(bank[3][:, 128 * i:128 * i + 128], gtokK[:, 128 * hd:128 * hd + 128], gUd[:, i, :],
                                                        start=True, stop=True)
                            last.then_inc(gs_raw, 1)
                            after(got_ready)
                            for i in range(GROUP):
                                last = nc.tensor.transpose(bank[7][:, 128 * i:128 * i + 128], gOt[:, i, :], ident)
                            last.then_inc(goT_raw, 1)
                            after(gs_ready)
                            after(goT_ready)
                        else:
                            for i in range(GROUP):
                                gdn_sample(g, i)
                for c in range(CH):
                    after(sub_squared)
                    nc.tensor.matmul(bank[c][:, 0:NT], ones, W(0)[:, c, :], start=True, stop=True).then_inc(sub_ssq, 1)
                after(sub_rms, 8)
                after(og_ready, 8)
                square(b + 9, W(GO_), 0, lambda d: None)

            def gdn_sample(g, i):
                hd = 4 * g + i
                after(gstate_in[hd % 2], 16)
                for b in range(DEC_B):
                    c0 = SEQ + DEC_T * b
                    last = nc.tensor.matmul(bank[0][:, 8 * b:8 * b + 8], gS0[:, hd % 2, b, :], work[:, 0:2, hd, c0:c0 + DEC_T],
                                            start=True, stop=True)
                last.then_inc(gst_raw, 1)
                after(gst_ready)
                for w in range(2):
                    last = nc.tensor.matmul(bank[1][0:NS, 128 * w:128 * w + 128], gST[:, w, :], ident, start=True, stop=True)
                last.then_inc(ks_raw, 1)
                after(r_ready)
                nc.tensor.matmul(bank[5][0:NS, 0:128], gXT[0:NS, i, 0:NS], gR[0:NS, i, :], start=True, stop=True).then_inc(w_raw, 1)
                after(gu_ready)
                nc.tensor.matmul(bank[6][0:NS, 0:128], aqk[0:NS, i, 0:NS], gU[0:NS, i, :], start=True, stop=True).then_inc(go2_raw, 1)
                after(gue_ready)
                for e in range(2):
                    last = nc.tensor.matmul(bank[2 + e][:, :], gtokK[0:NS, 128 * hd:128 * hd + 128],
                                            gUe[0:NS, 4 * e:4 * e + 4, :].rearrange("p b n -> p (b n)"), start=True, stop=True)
                last.then_inc(gs_raw, 1)
                after(got_ready)
                nc.tensor.transpose(bank[7][:, 0:NS], gOt[0:NS, i, :], ident[0:NS, 0:NS]).then_inc(goT_raw, 1)
                after(gs_ready)
                after(goT_ready)

            for s, (kind, n) in enumerate(stages):
                norm(s)
                if kind != "ffn":
                    pe.wait_ge(h_ready, 8 * (s + 1))
                b = unit_base[s]
                m = ffn_before[s]
                if kind == "attn":
                    attention(s)
                if kind == "gdn":
                    gdn(s)
                if kind == "rwkv":
                    rwkv(s, n)
                if kind == "ffn":
                    w0, parts = split_credit(s), PARTS * m
                    gate_up_unit(w0 + 1, FCH * m + 1, parts)
                    with pe.Fori(1, GU_UNITS) as i:
                        gate_up_unit(i * 2 + (w0 + 1), i * 2 + (FCH * m + 1))
                    with pe.Fori(0, 2) as i:
                        for j in range(4):
                            half = j % 2
                            for dc in range(2):
                                if half == 0:
                                    pe.wait_ge(x_updated, i * 4 + (8 * (s + 1) - 4 + 2 * (j // 2) + dc + 1))
                                pe.wait_ge(w_lo_ready, i * 8 + (w0 + FCH + 2 * j + dc + 1))
                                for k in range(11):
                                    if k == 0 and dc == 0 and j < 2:
                                        pe.wait_ge(act_lo_ready, parts + CH + 11 * (half + 1))
                                    last = three_products(bank[4 + 2 * (j // 2) + dc][:, 0:NT], w_hi[dc][:, k, :], w_lo[dc][:, k, :],
                                                          hid_hi[:, 11 * half + k, :], hid_lo[:, 11 * half + k, :],
                                                          half == 0 and k == 0, half == 1 and k == 10)
                                last.then_inc(half_done, 1)
            norm(len(stages))
            for c in range(CH):
                pe.wait_ge(h_ready, 8 * len(stages) + c + 1)
                if c >= 2:
                    pe.wait_ge(y_copied, 3 * (c - 1))
                for i, (t0, tn) in enumerate(TOK_TILES):
                    last = nc.tensor.transpose(bank[4 + c % 2 ][0:tn, 128 * i:128 * i + 128],
                                               h[:, c, t0:t0 + tn], ident[:, :])
                last.then_inc(y_transposed, 1)

        @block.scalar
        def _(act):
            def norm(k, meanwhile=lambda: None):
                for c in range(CH):
                    act.wait_ge(x_updated, 8 * k + c + 1)
                    nc.scalar.activation(h[:, c, :], x[:, c, :], ACT.Square).then_inc(squared, 1)
                meanwhile()
                act.wait_ge(ssq_done, k + 1)
                nc.scalar.activation(rms[:, :], bank[0][:, 0:NT], ACT.Sqrt, scale=1.0 / D, bias=eps_col[:, 0:1]).then_inc(rms_done, 1)

            act.wait_ge(consts_set, 4)
            after = follow(act)

            def high_part(u, e):
                raw, k = weight_piece(u, e)
                if e == 0:
                    act.wait_ge(slot_full[u % SLOTS], full(u))
                nc.scalar.copy(w_hi[e][:, 0:k, :], raw).then_inc(w_hi_ready, 1)

            def rwkv(s, j):
                b = unit_base[s]
                after(last_rows_transposed)
                for i in range(2):
                    nc.scalar.copy(shift_out[:, 512 * i:512 * i + 512], bank[6 - i][0:9, :]).then_inc(shift_out_ready, 1)

                jobs = [(64, lora_h[0:64, 0], ACT.Tanh, None), (64, lora_h[0:64, 1], ACT.Copy, None),
                        (128, lora_h[:, 2], ACT.Sigmoid, None), (32, lora_h[0:32, 3], ACT.Sigmoid, None)]
                if j:
                    jobs.append((32, lora_h[0:32, 4], ACT.Copy, None))
                    act.wait_ge(shift_out_stored, 16 * 2 * (j + 1))
                when = [HD(b, i + 1) for i in range(len(jobs))]
                second = [(SW_, ACT.Sigmoid, W0 + 8 * j), (A_, ACT.Sigmoid, A0 + 8 * j), (GATE_, ACT.Copy, None)]
                if j:
                    second.append((SV_, ACT.Sigmoid, V0))
                for i, (dst, fn, bias) in enumerate(second):
                    for d in range(8):
                        jobs.append((128, W(dst)[:, d, :], fn, None if bias is None else prm[:, bias + d:bias + d + 1]))
                        when.append(HD(b + 1, 8 * i + d + 1))
                for i, dst in enumerate((V_, R_, K_)):
                    for d in range(8):
                        jobs.append((128, W(dst)[:, d, :], ACT.Copy, None))
                        when.append(HD(b + 2 + 2 * i + d // 4, d % 4 // 2 + 1))
                for p, ((rows_, dst, fn, bias), w) in enumerate(zip(jobs, when)):
                    act.wait_ge(half_done, w)
                    src = bank[p % 8][0:rows_, 0:NT]
                    if bias is None:
                        nc.scalar.activation(dst, src, fn).then_inc(proj_evac, 1)
                    else:
                        nc.scalar.activation(dst, src, fn, bias=bias).then_inc(proj_evac, 1)

                after(cs_ready)
                nc.scalar.activation(W(P_), W(XX_), ACT.Exp).then_inc(p_ready, 1)
                nc.scalar.activation(W(PI_), W(XX_), ACT.Exp, scale=-1.0).then_inc(p_ready, 1)
                for c in range(CH):
                    after(kk_ssq)
                    nc.scalar.activation(W(LORA_)[:, c, :], bank[c][:, 0:NT], ACT.Sqrt, bias=eps_col[:, 1:2]).then_inc(kk_rms, 1)
                after(cs_prev_ready)
                nc.scalar.activation(W(AT_), W(XX_), ACT.Exp).then_inc(p_prev_ready, 1)

                for tile, (t0, tn) in enumerate(TOK_TILES):
                    for a, dst in ((0, tokV), (2, tokK)):
                        after(tok_transposed, 1 if a == 0 else 2)
                        for i in range(2):
                            last = nc.scalar.copy(dst[0:tn, 512 * i:512 * i + 512], bank[2 * a + i][0:tn, :])
                        last.then_inc(tok_ready_act, 1)
                    levels = 6 if tile < 2 else 2
                    for g in range(4):
                        ladder(tn, levels, Ym)
                        if tile < 2:
                            chunk_states(g, t0)
                        else:
                            for e in range(2):
                                sample_states(g, e)
                after(state_stored, 32)
                for c in range(CH):
                    after(centered)
                    nc.scalar.activation(W(PI_)[:, c, :], W(O_)[:, c, :], ACT.Square).then_inc(o_squared, 1)
                for c in range(CH):
                    after(var_raw)
                    nc.scalar.activation(W(PI_)[:, c, :], bank[c][:, 0:NT], ACT.Sqrt, scale=1.0 / DE,
                                         bias=eps_col[:, 2:3]).then_inc(sd_ready, 1)

            def ladder(tn, levels, Ym):
                for l in range(1, levels):
                    for e in range(2):
                        after(y_raw)
                        nc.scalar.copy(Ym[0:tn, 2 * e:2 * e + 2, 0:tn], pairs((4, 7)[e])[0:tn, 0, :, 0:tn]).then_inc(y_ready, 1)

            def chunk_states(g, t0):
                for ch in range(2):
                    r = slice(64 * ch, 64 * ch + 64)
                    after(rhs_raw)
                    nc.scalar.copy(Rhs[r, :], bank[7][r, 0:256]).then_inc(rhs_ready, 1)
                    after(u_raw)
                    nc.scalar.copy(Um[r, :], bank[7][r, 256:512]).then_inc(u_ready, 1)
                    after(ot_raw)
                    nc.scalar.copy(W(O_)[:, 2 * g:2 * g + 2, t0 + 64 * ch:t0 + 64 * ch + 64],
                                   bank4h[:, 0:2, 64 * ch:64 * ch + 64]).then_inc(o_copied, 1)

            def sample_states(g, e):
                after(s0_transposed)
                src = bank[0][:, :].rearrange("p (b n) -> p b n", n=64)
                nc.scalar.copy(Tbd[0:64, :, 0:64], src[0:64])
                nc.scalar.copy(Tbd[64:128, :, 64:128], src[64:128]).then_inc(t0_ready, 1)
                after(st_raw)
                nc.scalar.copy(ST[:, :, :].rearrange("p w (b t) -> p w b t", t=DEC_T),
                               bank[1][:, 0:64].rearrange("p (b w t) -> p w b t", w=2, t=DEC_T)).then_inc(st_ready, 1)
                after(rhs_raw)
                nc.scalar.copy(Rhs[0:NS, 0:128], bank[2][0:NS, 0:128]).then_inc(rhs_ready, 1)
                after(u_raw)
                nc.scalar.copy(Um[0:NS, 0:128], bank[2][0:NS, 128:256]).then_inc(u_ready, 1)
                after(state_transposed, 1)
                if g or e:
                    after(state_stored, 32)
                for i in range(2):
                    nc.scalar.copy(Sout[:, 4 * i:4 * i + 4, :], bank[5 + i][0:64, :].rearrange("p (b n) -> p b n", n=128)).then_inc(state_out_ready, 1)

            def attention(s):
                b = unit_base[s]
                for i, dst in enumerate((0, 1, 2)):
                    for d in range(8):
                        act.wait_ge(half_done, HD(b + 2 * i + d // 4, d % 4 // 2 + 1))
                        nc.scalar.activation(W(dst)[:, d, :], bank[d][:, 0:NT], ACT.Copy,
                                             scale=0.125 if i == 0 else 1.0).then_inc(proj_evac, 1)
                after(lam_sums)
                nc.scalar.activation(lam_tmp[:, 2:4], lam_tmp[:, 0:2], ACT.Exp).then_inc(lam_exp, 1)
                after(fb_raw)
                nc.scalar.copy(fbias, bank[0][0:AH, 0:FN]).then_inc(fb_ready, 1)
                after(sbias_raw)
                nc.scalar.copy(sbias[:, :], bank[1][:, 0:SK]).then_inc(sbias_ready, 1)
                for i, (t0, tn) in enumerate(TOK_TILES):
                    after(ktok_raw)
                    for e in range(2):
                        last = nc.scalar.copy(akey[0:tn, i, 512 * e:512 * e + 512], bank[2 + e][0:tn, :])
                    last.then_inc(ktok_ready, 1)
                jobs = [(hd, qt) for hd in range(AH) for qt in range(2)]

                def exps(n):
                    nk = 128 * (jobs[n][1] + 1)
                    after(max_ready)
                    for sub in range(2):
                        last = nc.scalar.activation(prob[:, n % 2, sub, 0:nk], bank[2 * (n % 2) + sub][:, 0:nk], ACT.Exp,
                                                    bias=neg_max[:, 2 * (n % 2) + sub:2 * (n % 2) + sub + 1],
                                                    accum_out=expsum[:, 2 * (n % 2) + sub:2 * (n % 2) + sub + 1])
                    last.then_inc(exp_ready, 1)

                def copy_probs(n):
                    k = jobs[n][1] + 1
                    after(probT_raw)
                    nc.scalar.copy(probT[:, n % 2, 0:k, :].rearrange("p k n -> p (k n)"), bank[4 + n % 2][:, 0:128 * k]).then_inc(probT_ready, 1)

                for n in range(len(jobs) + 1):
                    if n < len(jobs):
                        exps(n)
                    if n >= 1:
                        copy_probs(n - 1)
                for r in range(4):
                    for e in range(2):
                        after(pageT_raw)
                        for i in range(2):
                            last = nc.scalar.copy(scrA[:, 512 * i:512 * i + 512], bank[i][:, :])
                        last.then_inc(pageT_ready_act, 1)
                        after(pageT_raw)
                        after(sT_raw)
                        nc.scalar.copy(scoreT[:, :, 64 * e:64 * e + 64], bank[4][:, 0:128].rearrange("p (g r) -> p g r", g=2))
                        nc.scalar.copy(scoreNT[:, 64 * e:64 * e + 64], bank[5][0:NS, 0:64]).then_inc(sT_ready, 1)
                    after(s_biased)
                    nc.scalar.activation(sprob, sprob, ACT.Exp, bias=neg_max[:, 0:1], accum_out=expsum[:, 0:1]).then_inc(s_exp, 1)
                    after(sprobT_raw)
                    nc.scalar.copy(sprobT[:, 0:2, :].rearrange("p g r -> p (g r)"), bank[0][:, 0:256])
                    nc.scalar.copy(sprobT[0:NS, 2, :], bank[0][0:NS, 256:384]).then_inc(sprobT_ready, 1)
                after(sub_squared, 0)
                act.wait_ge(ao_ready, 20)
                for c in range(CH):
                    nc.scalar.activation(W(Q_)[:, c, :], W(AO_)[:, c, :], ACT.Square).then_inc(sub_squared, 1)
                for c in range(CH):
                    after(sub_ssq)
                    nc.scalar.activation(W(1)[:, c, :], bank[c][:, 0:NT], ACT.Sqrt, scale=1.0 / 128, bias=eps_col[:, 3:4]).then_inc(sub_rms, 1)

            def gdn(s):
                b = unit_base[s]
                after(pads_zeroed)
                act.wait_ge(half_done, HD(b, 1))
                nc.scalar.copy(graw[:, 0:2, :], bank[0][:, 0:32].rearrange("p (i n) -> p i n", n=16))
                nc.scalar.copy(graw[0:NS, 2, :], bank[0][0:NS, 32:48]).then_inc(proj_evac, 1)
                for c in range(24):
                    act.wait_ge(half_done, HD(b + 1 + c // 4, c % 4 // 2 + 1))
                    if c == 0:
                        act.wait_ge(prev_ready, 1)
                    if c >= 4:
                        act.wait_ge(conv_done, c - 3)
                        act.wait_ge(tail_done, c - 3)
                    src = bank[(1 + c) % 8]
                    xs = xp[:, c % 4, SEQ + 3:].rearrange("p (b t) -> p b t", t=7)
                    nc.scalar.copy(xs[:, :, 0:3], conv_prev[:, c, :].rearrange("p (b t) -> p b t", t=3)).then_inc(xp_ready, 1)
                    nc.scalar.copy(xp[:, c % 4, 3:SEQ + 3], src[:, 0:SEQ]).then_inc(xp_ready, 1)
                    nc.scalar.copy(xs[:, :, 3:7], src[:, SEQ:NT].rearrange("p (b t) -> p b t", t=DEC_T)).then_inc(proj_evac, 1)
                for c in range(CH):
                    act.wait_ge(half_done, HD(b + 7 + c // 4, c % 4 // 2 + 1))
                    nc.scalar.activation(W(GZ_)[:, c, :], bank[(25 + c) % 8][:, 0:NT], ACT.Silu).then_inc(proj_evac, 1)
                for c in range(24):
                    act.wait_ge(conv_done, c + 1)
                    nc.scalar.activation(W(c // 8)[:, c % 8, :], W(c // 8)[:, c % 8, :], ACT.Silu).then_inc(qkv_silu, 1)
                after(tails_raw)
                for i in range(6):
                    last = nc.scalar.copy(tail_rows[:, 512 * i:512 * i + 512], bank[i][0:27, :])
                last.then_inc(tail_rows_ready, 1)
                after(g_abs)
                nc.scalar.activation(gtmp[:, 0], gtmp[:, 0], ACT.Exp, scale=-1.0).then_inc(act_step, 1)
                nc.scalar.activation(gpar[:, 0, :], gpar[:, 0, :], ACT.Exp).then_inc(act_step, 1)
                act.wait_ge(act_step, 2)
                nc.scalar.activation(gtmp[:, 0], gtmp[:, 0], ACT.Ln, bias=ones[:, 0:1])
                nc.scalar.activation(gcol[:, BETA], graw[:, :, 0:8], ACT.Sigmoid).then_inc(g_ln, 1)
                for i in range(2):
                    for c in range(CH):
                        after(qk_ssq)
                        if i:
                            act.wait_ge(qk_ready, 1)
                        nc.scalar.activation(gsd[:, c, :], bank[c][:, 0:NT], ACT.Sqrt, bias=eps_col[:, 0:1]).then_inc(qk_rms, 1)
                after(gsum_ready)
                nc.scalar.activation(gcol[:, EGC], gcol[:, EGC], ACT.Exp)
                nc.scalar.activation(gcol[:, EDL], gcol[:, EDL], ACT.Exp)
                nc.scalar.activation(gcol[:, EGL], gcol[:, EGL], ACT.Exp)
                nc.scalar.activation(egLs, egLs, ACT.Exp).then_inc(gexp_ready, 1)
                act.wait_ge(gs_zeroed, 1)
                for tile, (t0, tn) in enumerate(TOK_TILES):
                    for a, dst in enumerate((gtokV, gtokK)):
                        after(gtok_raw)
                        for i in range(2):
                            last = nc.scalar.copy(dst[0:tn, 512 * i:512 * i + 512], bank[2 * a + i][0:tn, :])
                        last.then_inc(gtok_ready, 1)
                    levels = 7 if tile < 2 else 2
                    for g in range(2):
                        after(dec_raw)
                        src = bank[0][0:tn, :].rearrange("p (h n) -> p h n", n=128)[:, :, 0:tn]
                        nc.scalar.activation(gE[0:tn, :, 0:tn], src, ACT.Exp).then_inc(dec_ready, 1)
                        ladder(tn, levels, gY)
                        for i in range(GROUP):
                            hd = 4 * g + i
                            beta, bedl, egc = (gcol[0:tn, k, tile, hd:hd + 1] for k in (BETA, BEDL, EGC))
                            if tile < 2:
                                if i == 0:
                                    after(go1_raw)
                                    for q in range(GROUP):
                                        last = nc.scalar.activation(gOt[:, q, :], bank[4][:, 128 * q:128 * q + 128], ACT.Copy,
                                                                    scale=gcol[:, EGC, tile, 4 * g + q:4 * g + q + 1])
                                    last.then_inc(go1_ready, 1)
                                    after(w_raw)
                                nc.scalar.activation(gU[:, i, :], bank[5][:, 128 * i:128 * i + 128], ACT.Copy, scale=beta)
                                last = nc.scalar.activation(gUd[:, i, :], bank[5][:, 128 * i:128 * i + 128], ACT.Copy, scale=bedl)
                                if i == 3:
                                    last.then_inc(gu_ready, 1)
                                    after(goT_raw)
                                    nc.scalar.copy(W(GO_)[:, 4 * g:4 * g + 4, t0:t0 + tn],
                                                   bank[7][:, :].rearrange("p (h n) -> p h n", n=128)).then_inc(goT_ready, 1)
                            else:
                                after(gst_raw)
                                nc.scalar.copy(gST[:, :, :].rearrange("p w (b t) -> p w b t", t=DEC_T),
                                               bank[0][:, 0:64].rearrange("p (b w t) -> p w b t", w=2, t=DEC_T)).then_inc(gst_ready, 1)
                                after(w_raw)
                                nc.scalar.activation(gU[0:NS, i, :], bank[5][0:NS, 0:128], ACT.Copy, scale=beta)
                                nc.scalar.activation(gUd[0:NS, i, :], bank[5][0:NS, 0:128], ACT.Copy, scale=bedl).then_inc(gu_ready, 1)
                                after(goT_raw)
                                nc.scalar.copy(W(GO_)[:, hd, SEQ:], bank[7][:, 0:NS]).then_inc(goT_ready, 1)
                act.wait_ge(goT_ready, 4 + GH)
                for c in range(CH):
                    nc.scalar.activation(W(0)[:, c, :], W(GO_)[:, c, :], ACT.Square).then_inc(sub_squared, 1)
                for c in range(CH):
                    after(sub_ssq)
                    nc.scalar.activation(W(1)[:, c, :], bank[c][:, 0:NT], ACT.Sqrt, scale=1.0 / 128, bias=eps_col[:, 0:1]).then_inc(sub_rms, 1)

            for s, (kind, n) in enumerate(stages):
                m, b = ffn_before[s], unit_base[s]
                if kind != "ffn":
                    norm(s)
                if kind == "attn":
                    attention(s)
                if kind == "gdn":
                    gdn(s)
                if kind == "rwkv":
                    rwkv(s, n)
                if kind == "ffn":
                    def first_pieces():
                        for e in range(2):
                            high_part(b, e)
                    norm(s, first_pieces)
                    for c in range(CH):
                        act.wait_ge(h_ready, 8 * s + c + 1)
                        nc.scalar.copy(h_hi[:, c, :], h[:, c, :]).then_inc(act_hi_ready, 1)

                    for u in range(GU_UNITS):
                        for e in range(2):
                            act.wait_ge(half_done, HD(b + u, e + 1))
                            nc.scalar.activation(silu[:, e, :], bank[2 * e][:, 0:NT], ACT.Silu).then_inc(silu_done, 1)
                            high_part(b + u + 1, e)
                            act.wait_ge(gate_up_free, 2 + FCH * m + 2 * u + e + 1)
                            nc.scalar.copy(hid_hi[:, 2 * u + e, :], prod[:, e, :]).then_inc(act_hi_ready, 1)
                    for u in range(GU_UNITS, FFN_UNITS - 1):
                        for e in range(2):
                            act.wait_ge(half_done, HD(b + u, e + 1))
                            high_part(b + u + 1, e)
            norm(len(stages))

        @block.vector
        def _(dve):
            dve.wait_ge(prm_transposed, 1)
            nc.vector.tensor_copy(prm[:, 0:NROWS], bank[0][:, 0:NROWS]).then_inc(prm_ready, 1)
            for c in range(CH):
                dve.wait_ge(x_transposed, c + 1)
                nc.vector.tensor_copy(x[:, c, :], bank[4 + c % 4][:, 0:NT]).then_inc(x_updated, 1)
            dve.wait_ge(prm_ready, 1)

            def norm(k, g, parts=None):
                dve.wait_ge(rms_done, k + 1)
                nc.vector.reciprocal(rinv[:, :], rms[:, :]).then_inc(rinv_done, 1)
                dve.wait_ge(rinv_done, k + 1)
                for c in range(CH + 1):
                    if c < CH:
                        nc.vector.scalar_tensor_tensor(h[:, c, :], x[:, c, :], prm[:, g + c:g + c + 1], rinv[:, :],
                                                       ALU.mult, ALU.mult).then_inc(h_ready, 1)
                    if parts is not None and c:
                        dve.wait_ge(act_hi_ready, parts + c)
                        nc.vector.tensor_tensor(h_lo[:, c - 1, :], h[:, c - 1, :], h_hi[:, c - 1, :], ALU.subtract).then_inc(act_lo_ready, 1)

            def low_part(N, e, m):
                raw, k = weight_piece(N, e)
                owner = max(s for s in unit_base if unit_base[s] <= N)
                dve.wait_ge(w_hi_ready, PIECES * m + 2 * (N - unit_base[owner]) + e + 1)
                nc.vector.tensor_tensor(w_lo[e][:, 0:k, :], raw, w_hi[e][:, 0:k, :], ALU.subtract).then_inc(w_lo_ready, 1)

            after = follow(dve)
            steps = [0]

            def link(ins):
                steps[0] += 1
                ins.then_inc(dve_step, 1)
                dve.wait_ge(dve_step, steps[0])

            V = nc.vector
            TT = nc.vector.tensor_tensor

            def rwkv(s, j):
                b = unit_base[s]
                base = proj_before[s]
                dve.wait_ge(h_ready, 8 * (s + 1))
                V.tensor_copy(lastc[:, :, 0:1], h[:, :, SEQ - 1:SEQ])
                V.tensor_copy(lastc[:, :, 1:9], h[:, :, SEQ + DEC_T - 1:NT:DEC_T]).then_inc(last_cols_ready, 1)
                after(shift_transposed)
                link(V.tensor_copy(shift_cols[:, :, :], bank[7][:, 0:64].rearrange("p (c b) -> p c b", b=8)))
                xx, us = W(XX_), h[:, :, SEQ:].rearrange("p c (b t) -> p c b t", t=DEC_T)
                xs = xx[:, :, SEQ:].rearrange("p c (b t) -> p c b t", t=DEC_T)
                TT(xx[:, :, 1:SEQ], h[:, :, 0:SEQ - 1], h[:, :, 1:SEQ], ALU.subtract)
                V.tensor_scalar(xx[:, :, 0:1], h[:, :, 0:1], -1.0, None, ALU.mult)
                for i in range(1, DEC_T):
                    TT(xs[:, :, :, i], us[:, :, :, i - 1], us[:, :, :, i], ALU.subtract)
                link(TT(xs[:, :, :, 0], shift_cols[:, :, :], us[:, :, :, 0], ALU.subtract))
                for i, m in enumerate((1, 4, 5, 3, 0, 2)):
                    if i >= 2:
                        dve.wait_ge(half_done, (HD(b, 1), HD(b, 2), HD(b, 4), HD(b + 3, 2))[i - 2])
                    mu = MU + 8 * (6 * j + m)
                    for c in range(CH):
                        last = V.scalar_tensor_tensor(W((XM0_, XM1_)[i % 2])[:, c, :], xx[:, c, :], prm[:, mu + c:mu + c + 1],
                                                      h[:, c, :], ALU.mult, ALU.add)
                    last.then_inc(xm_ready, 1)

                dve.wait_ge(proj_evac, base + n_products(j))
                dve.wait_ge(shift_out_stored, 32 * (j + 1))
                after(xm_ready, 6)
                V.tensor_scalar(omka[:, :], prm[:, KAW + 8 * j:KAW + 8 * j + 8], -1.0, 1.0, ALU.mult, ALU.add)
                V.memset(Tbd, 0.0)
                V.memset(Rhs, 0.0)
                V.memset(Um, 0.0)
                link(V.tensor_scalar(W(SW_), W(SW_), -float(np.exp(-0.5)), None, ALU.mult))
                for c in range(CH):
                    last = V.tensor_tensor_scan(W(XX_)[:, c, :], reset, W(SW_)[:, c, :], 0.0, ALU.mult, ALU.add)
                last.then_inc(cs_ready, 1)
                link(TT(W(KN_), W(K_), by_feature(KKW + 8 * j), ALU.mult) if not j else V.memset(Ttmp, 0.0))
                if j:
                    after(vfirst_in, 16)
                    vf = W(BONUS_)
                    link(TT(vf, vf, W(V_), ALU.subtract))
                    link(TT(vf, vf, W(SV_), ALU.mult))
                    link(TT(W(V_), W(V_), vf, ALU.add))
                    link(TT(W(KN_), W(K_), by_feature(KKW + 8 * j), ALU.mult))
                TT(W(LORA_), W(KN_), W(KN_), ALU.mult).then_inc(kk_squared, 1)
                for c in range(CH):
                    last = V.tensor_scalar(W(BONUS_)[:, c, :], W(A_)[:, c, :], prm[:, KAW + 8 * j + c:KAW + 8 * j + c + 1],
                                           omka[:, c:c + 1], ALU.mult, ALU.add)
                link(last)
                link(TT(W(K_), W(K_), W(BONUS_), ALU.mult))
                link(TT(W(BONUS_), W(R_), W(K_), ALU.mult))
                TT(W(BONUS_), W(BONUS_), by_feature(RKW + 8 * j), ALU.mult).then_inc(rk_ready, 1)
                after(kk_rms, 8)
                link(V.reciprocal(W(LORA_), W(LORA_)))
                link(TT(W(KN_), W(KN_), W(LORA_), ALU.mult))
                for c in range(CH):
                    after(rk_sum)
                    TT(W(BONUS_)[:, c, :], bank[c][:, 0:NT], W(V_)[:, c, :], ALU.mult)
                after(p_ready, 2)
                TT(W(XX_), W(XX_), W(SW_), ALU.subtract).then_inc(cs_prev_ready, 1)
                TT(W(R_), W(R_), W(P_), ALU.mult)
                TT(W(K_), W(K_), W(PI_), ALU.mult)
                V.tensor_copy(PL, W(P_)[:, :, RC - 1:SEQ:RC])
                V.tensor_copy(PLs, W(P_)[:, :, SEQ + DEC_T - 1:NT:DEC_T])
                after(p_prev_ready)
                V.scalar_tensor_tensor(W(AT_), W(KN_), -1.0, W(AT_), ALU.mult, ALU.mult)
                link(TT(W(BT_), W(KN_), W(A_), ALU.mult))
                TT(W(BT_), W(BT_), W(PI_), ALU.mult).then_inc(mixed_ready, 1)

                for tile, (t0, tn) in enumerate(TOK_TILES):
                    after(tok_transposed, 2)
                    for i in range(2):
                        last = V.tensor_copy(tokB[0:tn, 512 * i:512 * i + 512], bank[2 + i][0:tn, :])
                    last.then_inc(tok_ready_dve, 1)
                    after(tok_transposed)
                    levels = 6 if tile < 2 else 2
                    am = Am if tile < 2 else Ams
                    strict, incl = (strict64, incl64) if tile < 2 else (strict4, incl4)
                    for g in range(4):
                        for i in range(4):
                            after(a_raw)
                            src = bank[i][0:tn, :].rearrange("p (k n) -> p k n", k=4)
                            TT(am[:, i, 0:2, :], src[:, 0:2, 0:tn], strict.unsqueeze(1).broadcast_to([tn, 2, tn]), ALU.mult)
                            last = TT(am[:, i, 2:4, :], src[:, 2:4, 0:tn], incl.unsqueeze(1).broadcast_to([tn, 2, tn]), ALU.mult)
                        last.then_inc(a_masked, 1)
                        after(a_masked)
                        ladder(tn, levels, am[:, :, 0, :], Xboth)
                        if tile < 2:
                            chunk_states(g, 2 * tile)
                        else:
                            for e in range(2):
                                sample_states(j, g, e)
                    if tile == 1:
                        after(prompt_state_transposed)
                        for i in range(2):
                            src = bank[i][:, :].rearrange("p (c n) -> p c n", n=128)
                            V.tensor_copy(Tst[0:64, 4 * i:4 * i + 4, :], src[0:64, :, 0:64])
                            last = V.tensor_copy(Tst[64:128, 4 * i:4 * i + 4, :], src[64:128, :, 64:128])
                        last.then_inc(state_out_ready_dve, 1)
                        link(V.memset(Tbd, 0.0))
                        V.memset(Ttmp, 0.0).then_inc(t0_zeroed, 1)
                after(state_transposed)
                for c in range(CH):
                    after(mean_raw)
                    V.scalar_tensor_tensor(W(O_)[:, c, :], bank[c][:, 0:NT], -1.0 / DE, W(O_)[:, c, :], ALU.mult, ALU.add).then_inc(centered, 1)
                for c in range(CH):
                    after(sd_ready)
                    link(V.reciprocal(W(PI_)[:, c, :], W(PI_)[:, c, :]))
                    link(TT(W(O_)[:, c, :], W(O_)[:, c, :], W(PI_)[:, c, :], ALU.mult))
                    lw, lb = LNW + 8 * j + c, LNB + 8 * j + c
                    link(V.tensor_scalar(W(O_)[:, c, :], W(O_)[:, c, :], prm[:, lw:lw + 1], prm[:, lb:lb + 1], ALU.mult, ALU.add))
                    link(TT(W(O_)[:, c, :], W(O_)[:, c, :], W(BONUS_)[:, c, :], ALU.add))
                    TT(W(O_)[:, c, :], W(O_)[:, c, :], W(GATE_)[:, c, :], ALU.mult).then_inc(og_ready, 1)
                if not j:
                    dve.wait_ge(v_stored, 16)
                add_to_x(b + 8)

            def add_to_x(unit):
                for c in range(CH):
                    dve.wait_ge(half_done, HD(unit + c // 4, c % 4 // 2 + 1))
                    TT(x[:, c, :], x[:, c, :], bank[c][:, 0:NT], ALU.add).then_inc(x_updated, 1)

            def ladder(tn, levels, nt, Xboth):
                many = lambda a: a.unsqueeze(1).broadcast_to([tn, GROUP, tn])
                xt = Xboth[0:tn, 1, :, 0:tn]
                link(TT(xt, nt, many(const("level0", tn, tn)), ALU.mult))
                TT(xt, xt, many(const("ident", tn, tn)), ALU.add).then_inc(xt_start, 1)
                for e in range(2):
                    after(x0_raw)
                    V.tensor_copy(Xboth[0:tn, 0, 2 * e:2 * e + 2, 0:tn], pairs((4, 7)[e])[0:tn, 0, :, 0:tn]).then_inc(x_ready, 1)
                for l in range(1, levels):
                    w = 0 if l < levels - 1 else 1
                    for e in range(2):
                        after(xy_raw)
                        both = Xboth[0:tn, w:2, 2 * e:2 * e + 2, 0:tn]
                        TT(both, both, pairs(5 + e)[0:tn, w:2, :, 0:tn], ALU.add).then_inc(x_ready, 1)

            def chunk_states(g, ch0):
                for ch in range(2):
                    after(ot_raw)
                    for e in range(2):
                        hp = 2 * g + e
                        pl = PL[:, hp, ch0 + ch:ch0 + ch + 1]
                        link(V.scalar_tensor_tensor(Ttmp, bank[5][:, 128 * e:128 * e + 128], pl, blk64, ALU.mult, ALU.mult))
                        last = V.scalar_tensor_tensor(Tbd[:, hp, :], Tbd[:, hp, :], pl, Ttmp, ALU.mult, ALU.add)
                        if e == 0:
                            link(last)
                    last.then_inc(t_ready, 1)

            def sample_states(jj, g, e):
                hp = 2 * g + e
                ue = lambda src: src.unsqueeze(1).broadcast_to([NS, DEC_B, 64])
                own = seq4.unsqueeze(2).broadcast_to([NS, DEC_B, 64])
                dve.wait_ge(u_ready, 24 * jj + 16 + hp + 1)
                for q in range(2):
                    if q:
                        after(st_new_raw)
                    TT(UE[:, 0], ue(Um[0:NS, 64 * q:64 * q + 64]), own, ALU.mult)
                    TT(UE[:, 1], ue(tokV[0:NS, 128 * hp + 64 * q:128 * hp + 64 * q + 64]), own, ALU.mult).then_inc(ue_ready, 1)
                    if q == 0:
                        after(so_raw)
                        TT(W(O_)[:, hp, SEQ:], bank[3][:, 0:NS], ST[:, 0, :], ALU.add)
                after(st_new_raw)
                if hp:
                    after(state_transposed)
                else:
                    after(prompt_state_stored, 32)
                src = bank[4][:, :].rearrange("p (b n) -> p b n", n=64)
                TT(Tst[0:64], Tbd[0:64, :, 0:64], src[0:64], ALU.add)
                link(TT(Tst[64:128], Tbd[64:128, :, 64:128], src[64:128], ALU.add))
                TT(Tst, Tst, PLs[:, hp, :].unsqueeze(2).broadcast_to([128, DEC_B, 64]), ALU.mult).then_inc(t_ready, 1)

            def attention(s):
                b = unit_base[s]
                after(attn_in, 48)
                link(TT(lamw[:, 0, :], lamw[:, 0, :], lamw[:, 1, :], ALU.mult))
                link(TT(lamw[:, 2, :], lamw[:, 2, :], lamw[:, 3, :], ALU.mult))
                V.reduce_sum(lam_tmp[:, 0:1], lamw[:, 0, :], axis=AX.X)
                V.reduce_sum(lam_tmp[:, 1:2], lamw[:, 2, :], axis=AX.X).then_inc(lam_sums, 1)
                after(lam_exp)
                link(TT(lam_col, lam_tmp[:, 2:3], lam_tmp[:, 3:4], ALU.subtract))
                link(V.tensor_scalar(lam_col, lam_col, LAM_INIT, None, ALU.add))
                link(TT(half_coef, acon_at("half1"), lam_col, ALU.mult))
                TT(half_coef, acon_at("half0"), half_coef, ALU.subtract)
                V.tensor_scalar(sub_col, prm[:, SUBLN:SUBLN + 1], 1.0 - LAM_INIT, None, ALU.mult)
                link(V.memset(rel_rows, 0.0))
                rr = rel_rows.rearrange("p i (e h u q) -> p i e h u q", e=2, h=AH, u=2)
                after(rel_const)
                for i in range(DEC_T):
                    for e in range(2):
                        last = V.tensor_copy(rr[:, i, e, :, :, i], rel_ext.unsqueeze(2).broadcast_to([BUCKETS + 1, AH, 2]))
                last.then_inc(rel_rows_ready, 1)
                for i, (t0, tn) in enumerate(TOK_TILES):
                    after(vtok_raw)
                    for e in range(2):
                        last = V.tensor_copy(aval[0:tn, i, 512 * e:512 * e + 512], bank[4 + e][0:tn, :])
                    last.then_inc(vtok_ready, 1)
                jobs = [(hd, qt) for hd in range(AH) for qt in range(2)]

                def maxima(n):
                    nk = 128 * (jobs[n][1] + 1)
                    after(score_raw)
                    c = 2 * (n % 2)
                    for sub in range(2):
                        last = V.tensor_reduce(neg_max[:, c + sub:c + sub + 1], bank[c + sub][:, 0:nk], axis=AX.X, op=ALU.max, negate=True)
                    last.then_inc(max_ready, 1)

                def difference(n):
                    nk = 128 * (jobs[n][1] + 1)
                    c = 2 * (n % 2)
                    after(exp_ready)
                    link(V.reciprocal(rcp[:, c:c + 2], expsum[:, c:c + 2]))
                    link(V.tensor_scalar(rcp[:, c + 1:c + 2], rcp[:, c + 1:c + 2], lam_col, -1.0, ALU.mult, ALU.mult))
                    pd = pdiff[:, n % 2, 0:nk]
                    link(V.tensor_scalar(pd, prob[:, n % 2, 0, 0:nk], rcp[:, c:c + 1], None, ALU.mult))
                    V.scalar_tensor_tensor(pd, prob[:, n % 2, 1, 0:nk], rcp[:, c + 1:c + 2], pd, ALU.mult, ALU.add).then_inc(diff_ready, 1)

                def copy_out(n):
                    hd, qt = jobs[n]
                    after(ao_raw)
                    V.tensor_copy(W(AO_)[:, hd, 128 * qt:128 * qt + 128], bank[6 + n % 2][:, 0:128]).then_inc(ao_ready, 1)

                for n in range(len(jobs) + 2):
                    if n < len(jobs):
                        maxima(n)
                    if n >= 2:
                        copy_out(n - 2)
                    if n < len(jobs):
                        difference(n)
                after(probT_raw, len(jobs))
                link(V.memset(q_split, 0.0))
                qs = W(Q_)[:, :, SEQ:].rearrange("p h (b t) -> p b h t", t=DEC_T)
                V.tensor_copy(q_split[0:64, :, :, 0:4], qs[0:64])
                V.tensor_copy(q_split[64:128, :, :, 4:8], qs[64:128]).then_inc(q_split_ready, 1)
                for r in range(4):
                    for e in range(2):
                        after(pageT_raw, 2)
                        for i in range(2, 4):
                            last = V.tensor_copy(scrA[:, 512 * i:512 * i + 512], bank[i][:, :])
                        last.then_inc(pageT_ready_dve, 1)
                    after(s_raw)
                    link(TT(sprob, bank[6][:, 0:SK], sbias[:, :], ALU.add))
                    link(TT(sprob[:, PAST:SK], sprob[:, PAST:SK], acon_at(f"other{r}"), ALU.add))
                    V.tensor_reduce(neg_max[:, 0:1], sprob, axis=AX.X, op=ALU.max, negate=True).then_inc(s_biased, 1)
                    after(s_exp)
                    link(V.reciprocal(rcp[:, 0:1], expsum[:, 0:1]))
                    link(TT(rcp[:, 1:2], rcp[:, 0:1], half_coef, ALU.mult))
                    V.tensor_scalar(sprob, sprob, rcp[:, 1:2], None, ALU.mult).then_inc(sprob_ready, 1)
                    after(sprobT_ready)
                    pv = sprobT.rearrange("p g (r u q) -> p g r u q", u=2, q=DEC_T)
                    dv = sdiffT.rearrange("p g (r q) -> p g r q", q=DEC_T)
                    TT(dv[:, 0:2], pv[:, 0:2, :, 0, :], pv[:, 0:2, :, 1, :], ALU.add)
                    TT(dv[0:NS, 2], pv[0:NS, 2, :, 0, :], pv[0:NS, 2, :, 1, :], ALU.add).then_inc(sdiff_ready, 1)
                    after(so2_raw)
                    V.tensor_copy(W(AO_)[:, :, SEQ + 8 * r:SEQ + 8 * r + 8].rearrange("p h (e q) -> p e h q", e=2),
                                  bank[7][:, 0:64].rearrange("p (e h q) -> p e h q", e=2, h=AH)).then_inc(ao_ready, 1)
                for c in range(CH):
                    after(sub_rms)
                    link(V.reciprocal(W(1)[:, c, :], W(1)[:, c, :]))
                    V.scalar_tensor_tensor(W(AO_)[:, c, :], W(AO_)[:, c, :], sub_col, W(1)[:, c, :], ALU.mult, ALU.mult).then_inc(og_ready, 1)
                dve.wait_ge(kv_stored, 16 * 6)
                add_to_x(b + 6)

            def gdn(s):
                b = unit_base[s]
                for i in range(4):
                    last = V.memset(xp[:, i, 0:3], 0.0)
                V.memset(graw, 0.0)
                V.memset(gcol[:, :, :, :], 0.0).then_inc(pads_zeroed, 1)
                after(prev_raw)
                for i in range(2):
                    last = V.tensor_copy(conv_prev[:, 12 * i:12 * i + 12, :].rearrange("p c n -> p (c n)"), bank[6 + i][:, 0:288])
                last.then_inc(prev_ready, 1)
                for c in range(24):
                    after(xp_ready, 2)
                    dve.wait_ge(proj_evac, proj_before[s] + 2 + c)
                    out = W(c // 8)[:, c % 8, :]
                    src = xp[:, c % 4, :]
                    outs = out[:, SEQ:].rearrange("p (b t) -> p b t", t=DEC_T)
                    srcs = src[:, SEQ + 3:].rearrange("p (b t) -> p b t", t=7)
                    for j in range(4):
                        w = prm[:, CONVW + 24 * j + c:CONVW + 24 * j + c + 1]
                        if j == 0:
                            V.tensor_scalar(out[:, 0:SEQ], src[:, 0:SEQ], w, None, ALU.mult)
                            link(V.tensor_scalar(outs, srcs[:, :, 0:4], w, None, ALU.mult))
                        else:
                            V.scalar_tensor_tensor(out[:, 0:SEQ], src[:, j:j + SEQ], w, out[:, 0:SEQ], ALU.mult, ALU.add)
                            last = V.scalar_tensor_tensor(outs, srcs[:, :, j:j + 4], w, outs, ALU.mult, ALU.add)
                            if j < 3:
                                link(last)
                            else:
                                last.then_inc(conv_done, 1)
                after(gpar_in, 32)
                xa = gcol[:, G_]
                dve.wait_ge(proj_evac, proj_before[s] + 1)
                link(TT(xa, graw[:, :, 8:16], gpar[:, 1, :].unsqueeze(1).broadcast_to([128, 3, 8]), ALU.add))
                link(V.tensor_scalar(gtmp[:, 0], xa, -1.0, None, ALU.mult))
                TT(gtmp[:, 0], gtmp[:, 0], xa, ALU.max).then_inc(g_abs, 1)
                after(g_ln)
                link(V.tensor_scalar(xa, xa, 0.0, None, ALU.max))
                link(TT(xa, xa, gtmp[:, 0], ALU.add))
                link(TT(xa, xa, gpar[:, 0, :].unsqueeze(1).broadcast_to([128, 3, 8]), ALU.mult))
                link(V.tensor_scalar(xa, xa, -1.0, None, ALU.mult))
                V.tensor_scalar(gcol[:, NBETA], gcol[:, BETA], -1.0, None, ALU.mult)
                TT(gGb[0:NS], gcol[0:NS, G_, 2, :].unsqueeze(1).broadcast_to([NS, DEC_B, 8]),
                   seq4.unsqueeze(2).broadcast_to([NS, DEC_B, 8]), ALU.mult).then_inc(g_ready, 1)
                dve.wait_ge(tail_rows_ready, 1)
                dve.wait_ge(conv_stored, 32)
                for i in range(2):
                    for c in range(CH):
                        if i:
                            after(qk_ssq)
                        dve.wait_ge(qkv_silu, 8 * i + c + 1)
                        TT(gsq[:, c, :], W(i)[:, c, :], W(i)[:, c, :], ALU.mult).then_inc(qk_squared, 1)
                    for c in range(CH):
                        after(qk_rms)
                        link(V.reciprocal(gsd[:, c, :], gsd[:, c, :]))
                        last = V.scalar_tensor_tensor(W(i)[:, c, :], W(i)[:, c, :], 128.0 ** -0.5 if i == 0 else 1.0, gsd[:, c, :],
                                                      ALU.mult, ALU.mult)
                    last.then_inc(qk_ready, 1)
                    if i == 0:
                        dve.wait_ge(qk_ready, 1)
                after(qk_ssq, 8)
                after(gsum_raw)
                for i, (t0, tn) in enumerate(TOK_TILES):
                    V.tensor_copy(gcol[0:tn, EGC, i, :], bank[0][0:tn, 8 * i:8 * i + 8])
                    V.tensor_copy(gcol[0:tn, EGL, i, :], bank[0][0:tn, 32 + 8 * i:40 + 8 * i])
                link(V.tensor_copy(egLs.rearrange("p b h -> p (b h)"), bank[0][:, 64:128]))
                TT(gcol[:, EDL], gcol[:, EGL], gcol[:, EGC], ALU.subtract).then_inc(gsum_ready, 1)
                dve.wait_ge(qk_ready, 2)
                V.memset(gS, 0.0).then_inc(gs_zeroed, 1)
                dve.wait_ge(qkv_silu, 24)
                after(gexp_ready)
                V.tensor_scalar(gcol[:, NEGC], gcol[:, EGC], -1.0, None, ALU.mult)
                link(TT(gcol[:, BEDL], gcol[:, BETA], gcol[:, EDL], ALU.mult))
                for tile, (t0, tn) in enumerate(TOK_TILES):
                    levels = 7 if tile < 2 else 2
                    strict, incl, later = (("strict128", "incl128", "after128") if tile < 2 else ("strict4", "incl4", "after4"))
                    strict, incl, later = (const(n_, tn) for n_ in (strict, incl, later))
                    over = lambda m: m.unsqueeze(1).broadcast_to([tn, GROUP, tn])
                    for g in range(2):
                        for i in range(GROUP):
                            last = V.tensor_scalar(gG[0:tn, i, 0:tn], later, gcol[0:tn, G_, tile, 4 * g + i:4 * g + i + 1], None, ALU.mult)
                        last.then_inc(g_spread, 1)
                        after(dec_ready)
                        E = gE[0:tn, :, 0:tn]
                        link(TT(E, E, over(incl), ALU.mult))
                        after(gram_raw)
                        TT(aqk[0:tn, :, 0:tn], bank[2][0:tn, :].rearrange("p (h n) -> p h n", n=128)[:, :, 0:tn], E, ALU.mult)
                        for i in range(GROUP):
                            last = V.scalar_tensor_tensor(gN[0:tn, i, 0:tn], bank[1][0:tn, 128 * i:128 * i + tn],
                                                          gcol[0:tn, NBETA, tile, 4 * g + i:4 * g + i + 1], gE[0:tn, i, 0:tn],
                                                          ALU.mult, ALU.mult)
                        link(last)
                        TT(gN[0:tn, :, 0:tn], gN[0:tn, :, 0:tn], over(strict), ALU.mult).then_inc(gn_masked, 1)
                        after(gn_masked)
                        ladder(tn, levels, gN[0:tn, :, 0:tn], gXboth)
                        for i in range(GROUP):
                            hd = 4 * g + i
                            negc = gcol[0:tn, NEGC, tile, hd:hd + 1]
                            tv = gtokV[0:tn, 128 * hd:128 * hd + 128]
                            if tile < 2:
                                if i == 0:
                                    after(ks_raw)
                                    dve.wait_ge(gtok_ready, 2 * tile + 2)
                                last = V.scalar_tensor_tensor(gR[:, i, :], bank[7][:, 128 * i:128 * i + 128], negc, tv, ALU.mult, ALU.add)
                                if i == 3:
                                    last.then_inc(r_ready, 1)
                                    after(go1_ready)
                                    after(go2_raw)
                                    TT(gOt, gOt, bank[6][:, :].rearrange("p (h n) -> p h n", n=128), ALU.add).then_inc(got_ready, 1)
                                    after(gs_raw)
                                    for q in range(GROUP):
                                        h2 = 4 * g + q
                                        last = V.scalar_tensor_tensor(gS[:, h2, :], gS[:, h2, :], gcol[:, EGL, tile, h2:h2 + 1],
                                                                      bank[3][:, 128 * q:128 * q + 128], ALU.mult, ALU.add)
                                    last.then_inc(gs_ready, 1)
                            else:
                                after(ks_raw)
                                if hd == 0:
                                    dve.wait_ge(gtok_ready, 6)
                                egc = gcol[0:NS, EGC, 2, hd:hd + 1]
                                V.tensor_scalar(gOt[0:NS, i, :], bank[1][0:NS, 0:128], egc, None, ALU.mult)
                                V.scalar_tensor_tensor(gR[0:NS, i, :], bank[1][0:NS, 128:256], negc, tv, ALU.mult, ALU.add).then_inc(r_ready, 1)
                                after(go2_raw)
                                dve.wait_ge(r_ready, 4 + hd + 1)
                                TT(gOt[0:NS, i, :], gOt[0:NS, i, :], bank[6][0:NS, 0:128], ALU.add).then_inc(got_ready, 1)
                                TT(gUe[0:NS], gUd[0:NS, i, :].unsqueeze(1).broadcast_to([NS, DEC_B, 128]),
                                   seq4.unsqueeze(2).broadcast_to([NS, DEC_B, 128]), ALU.mult).then_inc(gue_ready, 1)
                                after(gs_raw)
                                for q in range(DEC_B):
                                    last = V.scalar_tensor_tensor(gS0[:, hd % 2, q, :], gS0[:, hd % 2, q, :], egLs[:, q, hd:hd + 1],
                                                                  bank[2 + q // 4][:, 128 * (q % 4):128 * (q % 4) + 128], ALU.mult, ALU.add)
                                last.then_inc(gs_ready, 1)
                for c in range(CH):
                    after(sub_rms)
                    link(V.reciprocal(W(1)[:, c, :], W(1)[:, c, :]))
                    link(V.scalar_tensor_tensor(W(GO_)[:, c, :], W(GO_)[:, c, :], prm[:, GDNN:GDNN + 1], W(1)[:, c, :], ALU.mult, ALU.mult))
                    TT(W(GO_)[:, c, :], W(GO_)[:, c, :], W(GZ_)[:, c, :], ALU.mult).then_inc(og_ready, 1)
                for i in range(2):
                    dve.wait_ge(gstate_stored[i], 64)
                dve.wait_ge(gstate_p_stored, 16)
                add_to_x(b + 9)

            for s, (kind, n) in enumerate(stages):
                m = ffn_before[s]
                if kind == "attn":
                    norm(s, NORM + 8 * 4)
                    attention(s)
                if kind == "gdn":
                    norm(s, NORM + 8 * 7)
                    gdn(s)
                if kind == "rwkv":
                    norm(s, NORM + 8 * (3 * (3 * n) + 1))
                    rwkv(s, n)
                if kind == "ffn":
                    b = unit_base[s]
                    for e in range(2):
                        low_part(b, e, m)
                    norm(s, NORM + 8 * (3 * (n // 2) + 2 * (n % 2)), PARTS * m)
                    for u in range(GU_UNITS):
                        for e in range(2):
                            f = 2 * u + e
                            dve.wait_ge(silu_done, FCH * m + f + 1)
                            if f >= 2:
                                dve.wait_ge(act_lo_ready, PARTS * m + CH + f - 1)
                            nc.vector.tensor_tensor(prod[:, e, :], silu[:, e, :], bank[2 * e + 1][:, 0:NT], ALU.mult).then_inc(gate_up_free, 1)
                            low_part(b + u + 1, e, m)
                            dve.wait_ge(act_hi_ready, PARTS * m + CH + f + 1)
                            nc.vector.tensor_tensor(hid_lo[:, f, :], prod[:, e, :], hid_hi[:, f, :], ALU.subtract).then_inc(act_lo_ready, 1)
                    for u in range(GU_UNITS, FFN_UNITS):
                        v = u - GU_UNITS
                        for e in range(2):
                            if v % 2:
                                c = v // 2 * 2 + e
                                dve.wait_ge(half_done, HD(b + u, e + 1))
                                nc.vector.scalar_tensor_tensor(x[:, c, :], bank[4 + c % 4][:, 0:NT], 0.5, x[:, c, :],
                                                               ALU.mult, ALU.add).then_inc(x_updated, 1)
                            if u < FFN_UNITS - 1:
                                low_part(b + u + 1, e, m)
            norm(len(stages), FINAL)
            for c in range(CH):
                dve.wait_ge(y_transposed, c + 1)
                for i, (t0, tn) in enumerate(TOK_TILES):
                    nc.vector.tensor_copy(yout[0:tn, i, 128 * c:128 * c + 128],
                                          bank[4 + c % 2][0:tn, 128 * i:128 * i + 128]).then_inc(y_copied, 1)

        @block.gpsimd
        def _(pool):
            pool.dma_start(consts[:, :], t["consts"]).then_inc(consts_in, 16)
            for i in range(3):
                t0, tn = TOK_TILES[i]
                src = t["x_prompt"][0, t0:t0 + tn, :] if i < 2 else t["x_sample"].rearrange("b t d -> (b t) d")
                pool.dma_start(xin[0:tn, i, :], src).then_inc(x_in, 16)
            for src, i0, k, p0, n in row_loads:
                pool.dma_start(prm_rows[p0:p0 + n, k, :], src[i0:i0 + n, :]).then_inc(consts_in, 16)
            for i, e in enumerate((EPS, 1e-24, 64e-5, 1e-5)):
                nc.gpsimd.memset(eps_col[:, i:i + 1], e).then_inc(consts_set, 1)
            pool.sem_inc(gate_up_free, 2)
            pool.sem_inc(w_lo_ready, 2 * SLOTS)
            after = follow(pool)

            def rwkv_loads(s, j):
                pool.wait_ge(x_updated, 8 * (s + 1))
                pool.dma_start(shift_rows, t["state_rwkv_shift"][j]).then_inc(shift_in, 16)
                if j:
                    pool.wait_ge(v_stored, 16)
                    pool.dma_start(W(BONUS_), vfirst_dram).then_inc(vfirst_in, 16)

            def rwkv(s, j):
                base = proj_before[s]
                after(shift_out_ready, 2)
                pool.dma_start(t["rwkv_shift_p"][j], shift_out[0:1, :]).then_inc(shift_out_stored, 16)
                pool.dma_start(t["rwkv_shift_s"][j], shift_out[1:9, :]).then_inc(shift_out_stored, 16)
                if not j:
                    pool.wait_ge(proj_evac, base + 28 + 8)
                    pool.dma_start(vfirst_dram, W(V_)).then_inc(v_stored, 16)
                s0_src = t["state_rwkv_wkv"][j].rearrange("b h v k -> v b h k")
                s_dst = t["rwkv_wkv_s"][j].rearrange("b h v k -> v b h k")

                def load_s0(hp):
                    for e in range(2):
                        pool.dma_start(S0[:, :, 64 * e:64 * e + 64], s0_src[:, :, 2 * hp + e, :]).then_inc(s0_in, 16)

                for tile, (t0, tn) in enumerate(TOK_TILES):
                    levels = 6 if tile < 2 else 2
                    am = Am if tile < 2 else Ams
                    for g in range(4):
                        after(a_masked)
                        nl_levels(tn, levels, am[:, :, 0, :], NL)
                        if tile == 2:
                            for e in range(2):
                                hp = 2 * g + e
                                if hp:
                                    after(s0_transposed)
                                load_s0(hp)
                                after(state_out_ready, 2)
                                for e2 in range(2):
                                    pool.dma_start(s_dst[:, :, 2 * hp + e2, :], Sout[:, :, 64 * e2:64 * e2 + 64]).then_inc(state_stored, 16)
                    if tile == 1:
                        after(state_out_ready_dve)
                        dst = t["rwkv_wkv_p"][j, 0].rearrange("(c e) v k -> e v c k", e=2)
                        for e in range(2):
                            pool.dma_start(dst[e], Tst[64 * e:64 * e + 64, :, :]).then_inc(prompt_state_stored, 16)
                after(s0_transposed)

            def nl_levels(tn, levels, nt, NL):
                for l in range(1, levels):
                    nc.gpsimd.tensor_tensor(NL[0:tn, l - 1, :, 0:tn], nt,
                                            const(f"level{l}", tn, tn).unsqueeze(1).broadcast_to([tn, GROUP, tn]), ALU.mult)\
                      .then_inc(nl_ready, 1)

            def attention_loads(s):
                pool.wait_ge(x_updated, 8 * (s + 1))
                pool.dma_start(acon, t["attn_consts"]).then_inc(attn_in, 16)
                pool.dma_start(lamw.rearrange("p a n -> p (a n)"),
                               t["attn_lambda"][0].rearrange("a n -> (a n)").unsqueeze(0).broadcast_to([128, 256])).then_inc(attn_in, 16)
                pool.dma_start(rel_ext[0:BUCKETS], t["rel_bias"]).then_inc(attn_in, 16)
                pool.dma_start(page_ids[:, :], t["page_table"].rearrange("b g -> (b g)").unsqueeze(0)).then_inc(page_ids_in, 16)
                pool.wait_ge(page_ids_in, 16)
                pool.wait_ge(consts_set, 4)
                nc.gpsimd.memset(rel_ext[BUCKETS:BUCKETS + 1, :], NEG).then_inc(rel_const, 1)

            def load_pages(r, w):
                cache, arrived = (("cache_attn_k", kpage_in), ("cache_attn_v", vpage_in))[w]
                n_pool = t[cache].shape[1]
                for e in range(2):
                    for g in range(2):
                        i = 4 * r + 2 * e + g
                        page = nc.gpsimd.value_load(page_ids[0:1, i:i + 1], min_val=0, max_val=n_pool - 1)
                        src = t[cache][0].rearrange("g p h e -> g p (h e)")[bass.ds(page, 1)].rearrange("g p n -> (g p) n")
                        pool.dma_start(pages[:, w, e, g, :], src).then_inc(arrived[e] if w == 0 else arrived, 16)

            def attention(s):
                load_pages(0, 0)
                load_pages(0, 1)
                after(fb_ready)
                pool.dma_start(bias_dram, fbias).then_inc(fb_stored, 16)
                after(fb_stored, 16)
                window = bass.AP(tensor=bias_dram.tensor, offset=DEC_T, ap=[[1, 128], [FN, AH], [1, 256]])
                pool.dma_start(hankel, window).then_inc(hankel_in, 16)
                for i, (t0, tn) in enumerate(TOK_TILES):
                    for w, (name, ready) in enumerate((("attn_k", ktok_ready), ("attn_v", vtok_ready))):
                        after(ready)
                        if i < 2:
                            dst = t[name + "_p"][0, 0, t0:t0 + tn].rearrange("t h e -> t (h e)")
                        else:
                            dst = t[name + "_s"][0].rearrange("b t h e -> (b t) (h e)")
                        pool.dma_start(dst, ATOK[0:tn, w, i, :]).then_inc(kv_stored, 16)
                for r in range(1, 4):
                    pool.wait_ge(pageT_raw, 4 * r)
                    load_pages(r, 0)
                    pool.wait_ge(so2_raw, r)
                    load_pages(r, 1)

            def gdn_loads(s):
                pool.wait_ge(x_updated, 8 * (s + 1))
                pool.dma_start(conv_rows, t["state_gdn_conv"][0].rearrange("b j n -> (b j) n")).then_inc(conv_in, 16)
                for i, name in enumerate(("gdn_a_log", "gdn_dt_bias")):
                    pool.dma_start(gpar[:, i, :], t[name].broadcast_to([128, GH])).then_inc(gpar_in, 16)

            def gdn(s):
                src = t["state_gdn"][0].rearrange("b h k v -> h k b v")
                dst = t["gdn_state_s"][0].rearrange("b h k v -> h k b v")

                def load_state(hd):
                    pool.dma_start(gS0[:, hd % 2], src[hd]).then_inc(gstate_in[hd % 2], 16)

                load_state(0)
                load_state(1)
                for c in range(24):
                    pool.wait_ge(xp_ready, 2 * c + 2)
                    pool.wait_ge(proj_evac, proj_before[s] + 2 + c)
                    xs = xp[:, c % 4, SEQ + 3:].rearrange("p (b t) -> p b t", t=7)
                    nc.gpsimd.tensor_copy(tails[:, c, 0:3], xp[:, c % 4, SEQ:SEQ + 3])
                    nc.gpsimd.tensor_copy(tails[:, c, 3:27].rearrange("p (b t) -> p b t", t=3), xs[:, :, 4:7]).then_inc(tail_done, 1)
                after(tail_rows_ready)
                pool.dma_start(t["gdn_conv_p"][0, 0], tail_rows[0:3, :]).then_inc(conv_stored, 16)
                pool.dma_start(t["gdn_conv_s"][0].rearrange("b j n -> (b j) n"), tail_rows[3:27, :]).then_inc(conv_stored, 16)
                for tile, (t0, tn) in enumerate(TOK_TILES):
                    levels = 7 if tile < 2 else 2
                    for g in range(2):
                        after(gn_masked)
                        nl_levels(tn, levels, gN[0:tn, :, 0:tn], gNL)
                        if tile == 2:
                            for i in range(GROUP):
                                hd = 4 * g + i
                                pool.wait_ge(gs_ready, 4 + hd + 1)
                                pool.dma_start(dst[hd], gS0[:, hd % 2]).then_inc(gstate_stored[hd % 2], 16)
                                if hd + 2 < GH:
                                    pool.wait_ge(gstate_stored[hd % 2], 16 * (hd // 2 + 1))
                                    load_state(hd + 2)
                    if tile == 1:
                        pool.wait_ge(gs_ready, 4)
                        pool.dma_start(t["gdn_state_p"][0, 0].rearrange("h k v -> k h v"), gS).then_inc(gstate_p_stored, 16)
                for i in range(2):
                    pool.wait_ge(gstate_stored[i], 64)
                pool.wait_ge(gstate_p_stored, 16)

            for s, (kind, n) in enumerate(stages):
                if kind == "attn":
                    attention_loads(s)
                    attention(s)
                if kind == "gdn":
                    gdn_loads(s)
                    gdn(s)
                if kind == "rwkv":
                    rwkv_loads(s, n)
                    rwkv(s, n)
            pool.wait_ge(y_copied, 24)
            for i in range(3):
                t0, tn = TOK_TILES[i]
                dst = t["y_prompt"][0, t0:t0 + tn, :] if i < 2 else t["y_sample"].rearrange("b t d -> (b t) d")
                pool.dma_start(dst, yout[0:tn, i, :]).then_inc(stored, 16)
            pool.wait_ge(stored, 48)


STAGES = [("ffn", 0), ("rwkv", 0), ("ffn", 1), ("ffn", 2), ("attn", 0), ("ffn", 3),
          ("ffn", 4), ("gdn", 0), ("ffn", 5), ("ffn", 6), ("rwkv", 1), ("ffn", 7)]

INPUTS = ["x_prompt", "x_sample", "state_rwkv_wkv", "state_rwkv_shift", "cache_attn_k", "cache_attn_v", "state_gdn",
          "state_gdn_conv", "page_table", "norm_w", "final_norm_w", "ffn_w_gate", "ffn_w_up", "ffn_w_down", "rwkv_mu",
          "rwkv_w_rkv", "rwkv_w_o", "rwkv_w0", "rwkv_w1", "rwkv_w2", "rwkv_a0", "rwkv_a1", "rwkv_a2", "rwkv_g1", "rwkv_g2",
          "rwkv_k_k", "rwkv_k_a", "rwkv_r_k", "rwkv_lnx_w", "rwkv_lnx_b", "rwkv_v0", "rwkv_v1", "rwkv_v2", "attn_w_qkv",
          "attn_w_o", "attn_lambda", "attn_subln_w", "rel_bias", "gdn_w_in", "gdn_conv_w", "gdn_a_log", "gdn_dt_bias",
          "gdn_norm_w", "gdn_w_o"]

OUTPUTS = [("y_prompt", (1, SEQ, D)), ("y_sample", (DEC_B, DEC_T, D)),
           ("rwkv_wkv_p", (2, 1, RH, DE, DE)), ("rwkv_shift_p", (2, 1, D)),
           ("attn_k_p", (1, 1, SEQ, AH, 128)), ("attn_v_p", (1, 1, SEQ, AH, 128)),
           ("gdn_state_p", (1, 1, GH, 128, 128)), ("gdn_conv_p", (1, 1, 3, 3 * D)),
           ("rwkv_wkv_s", (2, DEC_B, RH, DE, DE)), ("rwkv_shift_s", (2, DEC_B, D)),
           ("attn_k_s", (1, DEC_B, DEC_T, AH, 128)), ("attn_v_s", (1, DEC_B, DEC_T, AH, 128)),
           ("gdn_state_s", (1, DEC_B, GH, 128, 128)), ("gdn_conv_s", (1, DEC_B, 3, 3 * D))]


def kernel(**inputs):
    from concourse.bass_utils import run_bass_kernel_spmd
    import concourse.bacc as bacc

    nc = bacc.Bacc("TRN2", target_bir_lowering=False, num_devices=1)
    arrays = {name: np.ascontiguousarray(inputs[name]) for name in INPUTS}
    arrays["consts"] = CONST_ARRAY
    arrays["attn_consts"] = ATTN_ARRAY
    t = {name: nc.dram_tensor(f"in_{name}", a.shape, mybir.dt.from_np(a.dtype), kind="ExternalInput").ap()
         for name, a in arrays.items()}
    for name, shape in OUTPUTS:
        t[name] = nc.dram_tensor(name, shape, mybir.dt.float32, kind="ExternalOutput").ap()
    program(nc, t, STAGES)
    r = run_bass_kernel_spmd(nc, [{f"in_{name}": a for name, a in arrays.items()}], core_ids=[0])
    return tuple(r.results[0][name] for name, _ in OUTPUTS)
```
